# Optimizing a Trainium2 kernel written in Bass

```python
import jax, jax.numpy as jnp
from jax import lax
import numpy as np

D_MODEL = 1024
BATCH = 1
SEQ = 1024
DEPTH = 1

CHUNK = 64
PLE_DIM = 256
RET_HEADS = 4
RET_QK_DIM = 64
RET_V_DIM = 128
RET_ROT_BASE = 10000.0
ATT_Q_HEADS = 8
ATT_KV_HEADS = 2
ATT_HEAD_DIM = 64
WINDOW = 128
WINDOW_CHUNKS = WINDOW // CHUNK
ROPE_THETA = 500000.0
ROPE_DIM = ATT_HEAD_DIM // 4
D_FF = 2816
CONV_WIDTH = 3
LN_EPS = 1e-5
RMS_EPS = 1e-6
NEG_INF = -1e30
ALPHA = (2.0 * DEPTH) ** 0.25
BETA = (8.0 * DEPTH) ** -0.25

RET_Q_W = RET_HEADS * RET_QK_DIM
RET_V_W = RET_HEADS * RET_V_DIM
ATT_Q_W = ATT_Q_HEADS * ATT_HEAD_DIM
ATT_KV_W = ATT_KV_HEADS * ATT_HEAD_DIM
IN_WIDTHS = (RET_Q_W, RET_Q_W, RET_V_W, RET_V_W, ATT_Q_W, ATT_KV_W, ATT_KV_W)
IN_SCALES = (1.0, 1.0, BETA, 1.0, 1.0, 1.0, BETA)
IN_SPLITS = tuple(int(s) for s in np.cumsum(IN_WIDTHS)[:-1])
IN_COLS = sum(IN_WIDTHS)
MIX_WIDTH = RET_V_W + ATT_Q_W

kernel_name = "hybrid_retention_swa_sink_layer"

def layer_norm(x, g, b):
    xf = x.astype(jnp.float32)
    mu = xf.mean(-1, keepdims=True)
    var = jnp.square(xf - mu).mean(-1, keepdims=True)
    return ((xf - mu) * lax.rsqrt(var + LN_EPS) * g + b).astype(x.dtype)

def rotary(t, pos, inv_freq, rot_dim):
    half = rot_dim // 2
    ang = pos.astype(jnp.float32)[:, :, None] * inv_freq
    cos = jnp.cos(ang)[:, :, None, :]
    sin = jnp.sin(ang)[:, :, None, :]
    tf = t.astype(jnp.float32)
    t1, t2 = tf[..., :half], tf[..., half:rot_dim]
    out = jnp.concatenate([t1 * cos - t2 * sin, t2 * cos + t1 * sin, tf[..., rot_dim:]], axis=-1)
    return out.astype(t.dtype)

def retention(q, k, v, g, pos):
    B, S = q.shape[:2]
    nc = S // CHUNK
    inv_freq = RET_ROT_BASE ** (-jnp.linspace(0.0, 1.0, RET_QK_DIM // 2, dtype=jnp.float32))
    q = rotary(q, pos, inv_freq, RET_QK_DIM)
    k = rotary(k, pos, inv_freq, RET_QK_DIM) * (RET_QK_DIM ** -0.5)
    log_gamma = jnp.log(1.0 - 2.0 ** (-5.0 - jnp.arange(RET_HEADS, dtype=jnp.float32)))
    idx = jnp.arange(CHUNK, dtype=jnp.float32)
    intra_decay = jnp.exp(log_gamma[:, None, None] * jnp.abs(idx[:, None] - idx[None, :]))
    key_decay = jnp.exp(log_gamma[None, :] * (CHUNK - 1.0 - idx)[:, None])
    query_decay = jnp.exp(log_gamma[None, :] * (idx + 1.0)[:, None])
    chunk_decay = jnp.exp(log_gamma * CHUNK)
    qc = q.reshape(B, nc, CHUNK, RET_HEADS, RET_QK_DIM)
    kc = k.reshape(B, nc, CHUNK, RET_HEADS, RET_QK_DIM)
    vc = v.reshape(B, nc, CHUNK, RET_HEADS, RET_V_DIM)
    scores = jnp.einsum('bnihd,bnjhd->bnhij', qc, kc) * intra_decay
    y_intra = jnp.einsum('bnhij,bnjhe->bnihe', scores, vc)
    kv = jnp.einsum('bnjhd,bnjhe->nbhde', kc * key_decay[:, :, None], vc)

    def step(state, kv_c):
        return state * chunk_decay[:, None, None] + kv_c, state

    _, prev = lax.scan(step, jnp.zeros(kv.shape[1:], kv.dtype), kv)
    y_cross = jnp.einsum('bnihd,nbhde->bnihe', qc * query_decay[:, :, None], prev)
    y = (y_intra + y_cross).astype(jnp.float32).reshape(B, S, RET_HEADS, RET_V_DIM)
    y = y * lax.rsqrt(jnp.mean(jnp.square(y), -1, keepdims=True) + RMS_EPS)
    return (jax.nn.silu(g.astype(jnp.float32)) * y).reshape(B, S, RET_V_W)

def sliding_window_sink_attention(q, k, v, sinks, pos):
    B, S = q.shape[:2]
    nc = S // CHUNK
    grp = ATT_Q_HEADS // ATT_KV_HEADS
    inv_freq = ROPE_THETA ** (-jnp.arange(ROPE_DIM // 2, dtype=jnp.float32) / (ROPE_DIM // 2))
    q = rotary(q, pos, inv_freq, ROPE_DIM)
    k = rotary(k, pos, inv_freq, ROPE_DIM)
    qc = q.reshape(B, nc, CHUNK, ATT_KV_HEADS, grp, ATT_HEAD_DIM)

    def band(t):
        t = t.reshape(B, nc, CHUNK, ATT_KV_HEADS, ATT_HEAD_DIM)
        parts = [jnp.pad(t, ((0, 0), (w, 0), (0, 0), (0, 0), (0, 0)))[:, :nc]
                 for w in range(WINDOW_CHUNKS - 1, -1, -1)]
        return jnp.concatenate(parts, axis=2)

    kb, vb = band(k), band(v)
    key_chunk = (jnp.arange(nc)[:, None] - (WINDOW_CHUNKS - 1)
                 + jnp.arange(WINDOW_CHUNKS * CHUNK)[None, :] // CHUNK)
    valid = key_chunk >= 0
    scores = jnp.einsum('bnikgd,bnjkd->bnkgij', qc, kb,
                        preferred_element_type=jnp.float32) * (ATT_HEAD_DIM ** -0.5)
    scores = jnp.where(valid[None, :, None, None, None, :], scores, NEG_INF)
    sink = sinks.astype(jnp.float32).reshape(1, 1, ATT_KV_HEADS, grp, 1, 1)
    m = jnp.maximum(scores.max(-1, keepdims=True), sink)
    e = jnp.exp(scores - m)
    probs = e / (e.sum(-1, keepdims=True) + jnp.exp(sink - m))
    out = jnp.einsum('bnkgij,bnjkd->bnikgd', probs.astype(vb.dtype), vb)
    return out.reshape(B, S, ATT_Q_W)

def hybrid_token_mixer(x, pos, w_in, w_out, sinks):
    B, S, _ = x.shape
    rq, rk, rv, rg, aq, ak, av = jnp.split(x @ w_in, IN_SPLITS, axis=-1)
    y_ret = retention(rq.reshape(B, S, RET_HEADS, RET_QK_DIM),
                      rk.reshape(B, S, RET_HEADS, RET_QK_DIM),
                      rv.reshape(B, S, RET_HEADS, RET_V_DIM),
                      rg.reshape(B, S, RET_HEADS, RET_V_DIM), pos)
    y_att = sliding_window_sink_attention(aq.reshape(B, S, ATT_Q_HEADS, ATT_HEAD_DIM),
                                          ak.reshape(B, S, ATT_KV_HEADS, ATT_HEAD_DIM),
                                          av.reshape(B, S, ATT_KV_HEADS, ATT_HEAD_DIM),
                                          sinks, pos)
    y = jnp.concatenate([y_ret.astype(x.dtype), y_att.astype(x.dtype)], axis=-1)
    return y @ w_out

def conv_ffn(x, w_up, conv_w, conv_b, w_down):
    u = x @ w_up
    u = lax.conv_general_dilated(u, conv_w[:, None, :].astype(u.dtype), (1,), [(CONV_WIDTH - 1, 0)],
                                 dimension_numbers=('NWC', 'WIO', 'NWC'),
                                 feature_group_count=2 * D_FF) + conv_b
    a, b = jnp.split(u, 2, axis=-1)
    return (jax.nn.gelu(a) * b) @ w_down

def setup_inputs(seed: int = 0) -> dict:
    key = jax.random.key(seed)
    ks = jax.random.split(key, 16)

    def nrm(k, shape, scale):
        return jax.random.normal(k, shape, jnp.float32) * scale

    x = nrm(ks[0], (BATCH, SEQ, D_MODEL), 1.0)
    p = nrm(ks[1], (DEPTH, BATCH, SEQ, PLE_DIM), 1.0)
    positions = (jax.random.randint(ks[2], (BATCH, 1), 0, 4096, jnp.int32)
                 + jnp.arange(SEQ, dtype=jnp.int32)[None, :])
    col_scale = jnp.concatenate([jnp.full((w,), s, jnp.float32) for w, s in zip(IN_WIDTHS, IN_SCALES)])
    w_in = nrm(ks[3], (DEPTH, D_MODEL, IN_COLS), D_MODEL ** -0.5) * col_scale
    w_out = nrm(ks[4], (DEPTH, MIX_WIDTH, D_MODEL), MIX_WIDTH ** -0.5 * BETA)
    attn_sinks = nrm(ks[5], (DEPTH, ATT_Q_HEADS), 0.5)
    ln1_g = 1.0 + nrm(ks[6], (DEPTH, D_MODEL), 0.02)
    ln1_b = nrm(ks[7], (DEPTH, D_MODEL), 0.02)
    w_up = nrm(ks[8], (DEPTH, D_MODEL, 2 * D_FF), D_MODEL ** -0.5)
    conv_w = nrm(ks[9], (DEPTH, CONV_WIDTH, 2 * D_FF), CONV_WIDTH ** -0.5)
    conv_b = nrm(ks[10], (DEPTH, 2 * D_FF), 0.02)
    w_down = nrm(ks[11], (DEPTH, D_FF, D_MODEL), D_FF ** -0.5 * BETA)
    ln2_g = 1.0 + nrm(ks[12], (DEPTH, D_MODEL), 0.02)
    ln2_b = nrm(ks[13], (DEPTH, D_MODEL), 0.02)
    w_ple_gate = nrm(ks[14], (DEPTH, D_MODEL, D_MODEL), D_MODEL ** -0.5)
    w_ple_proj = nrm(ks[15], (DEPTH, PLE_DIM, D_MODEL), PLE_DIM ** -0.5)
    return {"x": x, "p": p, "positions": positions, "w_in": w_in, "w_out": w_out,
            "attn_sinks": attn_sinks, "ln1_g": ln1_g, "ln1_b": ln1_b, "w_up": w_up,
            "conv_w": conv_w, "conv_b": conv_b, "w_down": w_down, "ln2_g": ln2_g,
            "ln2_b": ln2_b, "w_ple_gate": w_ple_gate, "w_ple_proj": w_ple_proj}

def reference(x, p, positions, w_in, w_out, attn_sinks, ln1_g, ln1_b, w_up, conv_w, conv_b,
              w_down, ln2_g, ln2_b, w_ple_gate, w_ple_proj):
    h = x
    for i in range(DEPTH):
        mix = hybrid_token_mixer(h, positions, w_in[i], w_out[i], attn_sinks[i])
        h = layer_norm(ALPHA * h + mix, ln1_g[i], ln1_b[i])
        h = layer_norm(ALPHA * h + conv_ffn(h, w_up[i], conv_w[i], conv_b[i], w_down[i]),
                       ln2_g[i], ln2_b[i])
        gate = jax.nn.sigmoid(h @ w_ple_gate[i])
        h = h + gate * (p[i] @ w_ple_proj[i])
    return h


_drawn_inputs = setup_inputs


def setup_inputs(seed=0):
    import zlib

    import numpy as np

    out = dict(_drawn_inputs(seed))
    spreads = {}
    factors = {'attn_sinks': 8.0,
     'ln1_g': 2.9,
     'ln1_b': 3.079,
     'conv_b': 7.234,
     'ln2_g': 3.214,
     'ln2_b': 3.055}
    for name, (base, spread) in spreads.items():
        noise = np.random.default_rng([zlib.crc32(name.encode()), seed]).standard_normal(out[name].shape)
        drawn = base * np.exp(spread * noise) if base else spread * noise
        out[name] = __import__('jax').numpy.asarray(drawn.astype(out[name].dtype))
    for name, factor in factors.items():
        out[name] = (out[name] * factor).astype(out[name].dtype)
    return out
```

```python
import numpy as np
import concourse.bass as bass
from concourse import mybir
from contextlib import ExitStack

P = 128
TOKENS = 1024
MODEL = 1024
NT = TOKENS // P
NK = MODEL // P
CHUNK = 64
RET_HEADS, RET_QK, RET_V = 4, 64, 128
Q_HEADS, KV_HEADS, HEAD = 8, 2, 64
PLE = 256
FF = 2816
NF = FF // P
PAIRS = NF // 2
ROPE_DIM = HEAD // 4
HALF_R, HALF_A = RET_QK // 2, ROPE_DIM // 2
NFREQ = HALF_R + HALF_A
ALPHA = 2.0 ** 0.25
LN_EPS, RMS_EPS = 1e-5, 1e-6
W = 512
ANGLE_MAGIC = 1.5 * 2.0 ** 23
TWO_PI = (6.28125, 1.9340515136718750e-3, 1.2551362e-6)
PI_BELOW = 3.1415925

C_DECAY, C_IDENT = 0, RET_HEADS * P
C_QDEC = C_IDENT + P
C_KDEC = C_QDEC + RET_HEADS
C_SDEC = C_KDEC + RET_HEADS
C_FREQ = C_SDEC + 2
C_MHALF = C_FREQ + NFREQ
C_END = C_MHALF + RET_HEADS

BLOCKS = ("qk", "v", "akv", "gate", "aq", "out0", "out1")
COLS = {"qk": 512, "v": 512, "akv": 256, "gate": 512, "aq": 512, "out0": 512, "out1": 512}
RING, RAWS = 12, 4


def build(nc, xT, x, pT, pos, w_in, w_out, sinks, ln, ff_up, ff_down, conv, w_gate, w_ple, cst_in, out):
    fp32, f32r = mybir.dt.float32, mybir.dt.float32r
    ALU, ACT, AX = mybir.AluOpType, mybir.ActivationFunctionType, mybir.AxisListType
    ctx = ExitStack()
    with ctx:
        base = nc.sbuf_base + (-nc.sbuf_base) % 64

        def at(name, offset, shape, dt=fp32):
            return nc.alloc_sbuf_tensor_at(name, [P] + list(shape), dt, offset=base + offset)

        KB = 1024
        actT_hi = at("actT_hi", 0, [NK, TOKENS], f32r)
        actT_lo = at("actT_lo", 32 * KB, [NK, TOKENS], f32r)
        RES = 64 * KB
        xT_raw = at("xT_raw", RES, [NK, TOKENS])
        rqk = at("rqk", RES, [NT, 512])
        rvy = at("rvy", RES + 16 * KB, [NT, 512])
        res = at("res", RES, [2, NT, W])
        RNG = 96 * KB
        ring_hi = at("ring_hi", RNG, [RING, W], f32r)
        ring_lo = at("ring_lo", RNG + 24 * KB, [RING, W], f32r)
        down_hi = at("down_hi", RNG, [2, MODEL], f32r)
        down_lo = at("down_lo", RNG + 24 * KB, [2, MODEL], f32r)
        gT_hi = at("gT_hi", RNG + 8 * KB, [2, TOKENS], f32r)
        gT_lo = at("gT_lo", RNG + 32 * KB, [2, TOKENS], f32r)
        up1_hi = at("up1_hi", RNG + 16 * KB, [NK, 256], f32r)
        up1_lo = at("up1_lo", RNG + 40 * KB, [NK, 256], f32r)
        pT_hi = at("pT_hi", RNG, [2, TOKENS], f32r)
        pT_lo = at("pT_lo", RNG + 24 * KB, [2, TOKENS], f32r)
        ple_hi = at("ple_hi", RNG + 8 * KB, [2, MODEL], f32r)
        ple_lo = at("ple_lo", RNG + 32 * KB, [2, MODEL], f32r)
        gw1_hi = at("gw1_hi", RNG + 16 * KB, [4, W], f32r)
        gw1_lo = at("gw1_lo", RNG + 40 * KB, [4, W], f32r)
        RAW = 144 * KB
        w_raw = at("w_raw", RAW, [RAWS, W])
        conv_ab = at("conv_ab", RAW, [2, TOKENS])
        pT_raw = at("pT_raw", RAW, [2, TOKENS])
        sig = at("sig", RAW, [2, W])
        outs = at("outs", RAW + 4 * KB, [2, W])
        M = 152 * KB
        cst = at("cst", M, [C_END])
        M += C_END * 4 + (-C_END * 4) % 64
        small = at("small", M, [256])
        M += 1024
        convp = at("convp", M, [NF, 8])
        M += NF * 32
        MIX = M
        sizes = {}

        def mix(name, shape, dt=fp32):
            sizes[name] = MIX + sizes.get("end", 0)
            t = at(name, sizes[name], shape, dt)
            sizes["end"] = sizes.get("end", 0) + int(np.prod(shape)) * 4
            return t

        kT_att = mix("kT_att", [KV_HEADS, TOKENS])
        akv = mix("akv", [NT, 256])
        v_even = mix("v_even", [NT, P])
        trig = mix("trig", [2, NT, NFREQ])
        probs = mix("probs", [2, 4, P])
        rot = at("rot", sizes["probs"], [2, 512])
        arot = mix("arot", [2, 8 * 2 * HALF_A])
        probsT = mix("probsT", [2, 4, P])
        kT_ret = at("kT_ret", sizes["probsT"], [2, P])
        kdec = at("kdec", sizes["probsT"] + KB, [256])
        score = at("score", sizes["probsT"] + 2 * KB, [RET_HEADS, P])
        qT_ret = mix("qT_ret", [2, 2, 2, P])
        stage = mix("stage", [2, W])
        assert MIX + 32 * KB <= sizes["stage"] <= MIX + 36 * KB
        state = mix("state", [2, 2, 256])
        qT_att = mix("qT_att", [2, 4, CHUNK])
        square = at("square", sizes["qT_att"], [512])
        aq = mix("aq", [2, 512])
        up_raw = at("up_raw", MIX, [2, NK * 256])
        up0_hi = at("up0_hi", MIX + 16 * KB, [NK, 256], f32r)
        up0_lo = at("up0_lo", MIX + 24 * KB, [NK, 256], f32r)
        down_raw = at("down_raw", MIX + 32 * KB, [2, MODEL])
        gains = at("gains", MIX + 40 * KB, [2, 2, W])
        gate_raw = at("gate_raw", MIX, [8, W])
        gw0_hi = at("gw0_hi", MIX + 16 * KB, [4, W], f32r)
        gw0_lo = at("gw0_lo", MIX + 24 * KB, [4, W], f32r)
        ple_raw = at("ple_raw", MIX + 32 * KB, [2, MODEL])

        decayT = cst[:, C_DECAY:C_IDENT].rearrange("p (h i) -> p h i", h=RET_HEADS)
        ident = cst[:, C_IDENT:C_QDEC]
        q_decay, k_decay = cst[:, C_QDEC:C_KDEC], cst[:, C_KDEC:C_SDEC]
        state_decay = cst[:, C_SDEC:C_FREQ]
        freq = cst[:, C_FREQ:C_MHALF]
        minus_half = cst[:, C_MHALF:C_END]
        cos_r, sin_r = trig[:, 0, :, 0:HALF_R], trig[:, 1, :, 0:HALF_R]
        cos_a, sin_a = trig[:, 0, :, HALF_R:NFREQ], trig[:, 1, :, HALF_R:NFREQ]

        posi = small[:, 0:8]
        posf = small[:, 8:16]
        sink = small[:, 16:20]
        rms_in = small[:, 24:28]
        rms = small[:, 32:40].rearrange("p (s h) -> p s h", s=2)
        smax = small[:, 40:48].rearrange("p (e b) -> p e b", e=2)
        sneg = small[:, 48:56].rearrange("p (e b) -> p e b", e=2)
        ssum = small[:, 56:64].rearrange("p (e b) -> p e b", e=2)
        sinkd = small[:, 64:72].rearrange("p (e b) -> p e b", e=2)
        sinke = small[:, 72:80].rearrange("p (e b) -> p e b", e=2)
        srec = small[:, 80:88].rearrange("p (e b) -> p e b", e=2)
        bnst = small[:, 96:120].rearrange("p (s n) -> p s n", s=2)
        mean = small[:, 128:144].rearrange("p (t n) -> p t n", t=NT)
        vare = small[:, 144:152]
        rstd = small[:, 152:160]
        nbias = small[:, 160:168]
        rsum = small[:, 168:176].rearrange("p (s h) -> p s h", s=2)

        psum = [ctx.enter_context(nc.psum_tensor(f"pair{j}", [P, 2 * W], fp32)) for j in range(4)]

        def bank(b):
            return psum[b // 2][:, (b % 2) * W:(b % 2 + 1) * W]

        def sem(name):
            return ctx.enter_context(nc.semaphore(name))

        cst_in_s, pos_in_s, conv_in_s = sem("cst_in"), sem("pos_in"), sem("conv_in")
        xT_in = [sem(f"xT_in{k}") for k in range(NK)]
        w_in_s = [sem(f"w_in{j}") for j in range(RAWS)]
        xres_in = [sem(f"xres_in{j}") for j in range(2)]
        gains_in = sem("gains_in")
        up_in = [sem(f"up_in{f}") for f in range(2)]
        down_in = [sem(f"down_in{f}") for f in range(2)]
        gate_in = [sem(f"gate_in{j}") for j in range(8)]
        ple_in = sem("ple_in")
        out_s = [sem(f"out{j}") for j in range(2)]
        x_hi, x_lo = sem("x_hi"), sem("x_lo")
        w_hi, w_lo, w_used = sem("w_hi"), sem("w_lo"), sem("w_used")
        dense = sem("dense")
        taken = sem("taken")
        res_done = sem("res_done")
        dve_s = sem("dve")
        angle_s, sine_s, rot_s, arotk_s, arotq_s = (sem(n) for n in ("angle", "sine", "rot", "arotk", "arotq"))
        zero_s = sem("zero")
        rT, rT_out, kd_s, r_score, r_decayed, r_kv, r_state, r_y, r_yout, r_sq, r_gated = (
            sem(n) for n in ("rT", "rT_out", "kd", "r_score", "r_decayed", "r_kv", "r_state", "r_y",
                             "r_yout", "r_sq", "r_gated"))
        r_ms, r_rms = sem("r_ms"), sem("r_rms")
        akT, akT_out, veven_s = sem("akT"), sem("akT_out"), sem("veven")
        aqT, aqT_out, a_score, a_max, a_exp, a_prob, a_pT, a_pT_out, a_y = (
            sem(n) for n in ("aqT", "aqT_out", "a_score", "a_max", "a_exp", "a_prob", "a_pT", "a_pT_out", "a_y"))
        a_hi, a_lo, m_T, m_hi, m_lo = (sem(n) for n in ("a_hi", "a_lo", "m_T", "m_hi", "m_lo"))
        n_var, n_rstd, n_bias, n_z, n_gain, n_h, n_T, n_hi, n_lo, n_alpha = (
            sem(n) for n in ("n_var", "n_rstd", "n_bias", "n_z", "n_gain", "n_h", "n_T", "n_hi", "n_lo", "n_alpha"))
        up_hi_s, up_lo_s, dn_hi_s, dn_lo_s = (sem(n) for n in ("up_hi", "up_lo", "dn_hi", "dn_lo"))
        u_done, c_init, c_done, gelu_s, g_mul, g_hi, g_lo, d_done, d_added = (
            sem(n) for n in ("u_done", "c_init", "c_done", "gelu", "g_mul", "g_hi", "g_lo", "d_done", "d_added"))
        gw_hi, gw_lo, gw_used, pl_hi, pl_lo, pl_done, gt_done, sig_s, gt_mul, gt_add = (
            sem(n) for n in ("gw_hi", "gw_lo", "gw_used", "pl_hi", "pl_lo", "pl_done", "gt_done", "sig",
                             "gt_mul", "gt_add"))

        def f32(ap):
            return ap.bitcast(fp32)

        items = [(b, k) for b in BLOCKS for k in range(NK)]
        first_unit = {b: j * NT for j, b in enumerate(BLOCKS)}
        N_ACT_UNITS = 5 * NT
        OUT0, OUT1 = first_unit["out0"], first_unit["out1"]

        def tok(t, n=P):
            return slice(t * P, t * P + n)

        up_hi_t, up_lo_t = (up0_hi, up1_hi), (up0_lo, up1_lo)
        gw_hi_t, gw_lo_t = (gw0_hi, gw1_hi), (gw0_lo, gw1_lo)
        block = ctx.enter_context(nc.Block())

        @block.sync
        def _(sp):
            def weight(n):
                b, k = items[n]
                c = COLS[b]
                if n >= RAWS:
                    sp.wait_ge(w_lo, n - RAWS + 1)
                if b.startswith("out"):
                    src = w_out[k * P:(k + 1) * P, int(b[3]) * W:(int(b[3]) + 1) * W]
                else:
                    c0 = sum(COLS[x] for x in BLOCKS[:BLOCKS.index(b)])
                    src = w_in[k * P:(k + 1) * P, c0:c0 + c]
                sp.dma_start(w_raw[:, n % RAWS, 0:c], src).then_inc(w_in_s[n % RAWS], 16)

            def residual(u):
                if u >= 2:
                    sp.wait_ge(res_done, u - 1)
                else:
                    sp.wait_ge(r_gated, NT)
                sp.dma_start(stage[:, u % 2, :], x[tok(u % NT), (u // NT) * W:(u // NT + 1) * W])\
                    .then_inc(xres_in[u % 2], 16)

            for k in range(NK):
                sp.dma_start(xT_raw[:, k, :], xT[k * P:(k + 1) * P, :]).then_inc(xT_in[k], 16)
                weight(k)
                if k == 2:
                    sp.dma_start(cst[:, :], cst_in).then_inc(cst_in_s, 16)
                    sp.dma_start(posi.bitcast(mybir.dt.int32), pos).then_inc(pos_in_s, 16)
                    sp.dma_start(sink, sinks).then_inc(pos_in_s, 16)
                    sp.dma_start(convp[:, :, :], conv).then_inc(conv_in_s, 16)
            for n in range(NK, OUT1):
                weight(n)
            residual(0)
            residual(1)
            for n in range(OUT1, OUT1 + 4):
                weight(n)
            for u in range(2, NT):
                residual(u)
            for n in range(OUT1 + 4, OUT1 + NK):
                weight(n)
            sp.wait_ge(a_lo, NT)
            for j in range(2):
                sp.dma_start(gains[:, j, :, :], ln[j].partition_broadcast(P)).then_inc(gains_in, 16)
            residual(NT)
            residual(NT + 1)
            for f in range(2):
                sp.dma_start(up_raw[:, f, :], ff_up[f]).then_inc(up_in[f], 16)
            for u in range(NT + 2, 2 * NT):
                residual(u)
            sp.wait_ge(res_done, 2 * NT)
            for f in range(2):
                sp.dma_start(down_raw[:, f, :], ff_down[f]).then_inc(down_in[f], 16)
            sp.wait_ge(n_h, NT)
            for j in range(2):
                sp.dma_start(gains[:, j, :, :], ln[2 + j].partition_broadcast(P)).then_inc(gains_in, 16)
            with sp.Fori(1, PAIRS) as i:
                for f in range(2):
                    sp.wait_ge(up_lo_s, i * 2 + (f - 1))
                    sp.dma_start(up_raw[:, f, :], ff_up[bass.ds(i * 2 + f, 1), :, :].rearrange("o p n -> (o p) n")).then_inc(up_in[f], 16)
                for f in range(2):
                    sp.wait_ge(dn_lo_s, i * 2 + (f - 1))
                    sp.dma_start(down_raw[:, f, :], ff_down[bass.ds(i * 2 + f, 1), :, :].rearrange("o p n -> (o p) n")).then_inc(down_in[f], 16)
            sp.wait_ge(up_lo_s, 2 * PAIRS)
            for k in range(NK):
                sp.dma_start(gate_raw[:, k, :], w_gate[k * P:(k + 1) * P, 0:W]).then_inc(gate_in[k], 16)
            sp.wait_ge(dn_lo_s, 2 * PAIRS)
            for k in range(2):
                sp.dma_start(ple_raw[:, k, :], w_ple[k * P:(k + 1) * P, :]).then_inc(ple_in, 16)
            sp.wait_ge(g_lo, 2 * PAIRS)
            for k in range(2):
                sp.dma_start(pT_raw[:, k, :], pT[k * P:(k + 1) * P, :]).then_inc(ple_in, 16)
            for k in range(NK):
                sp.wait_ge(gw_lo, k + 1)
                sp.dma_start(gate_raw[:, k, :], w_gate[k * P:(k + 1) * P, W:2 * W]).then_inc(gate_in[k], 16)
            for u in range(2 * NT):
                h, t = divmod(u, NT)
                sp.wait_ge(gt_add, u + 1)
                sp.dma_start(out[tok(t), h * W:(h + 1) * W], outs[:, u % 2, :]).then_inc(out_s[u % 2], 16)
            for j in range(2):
                sp.wait_ge(out_s[j], 16 * NT)

        @block.tensor
        def _(pe):
            mm = nc.tensor.matmul

            def three(dst, a_h, a_l, b_h, b_l, first, last):
                mm(dst, a_h, b_h, start=first, stop=False)
                mm(dst, a_h, b_l, start=False, stop=False)
                return mm(dst, a_l, b_h, start=False, stop=last)

            def product(u, k, dst, n):
                t, c = u % NT, COLS[items[n][0]]
                return three(dst[:, 0:c], actT_hi[:, k, tok(t)], actT_lo[:, k, tok(t)],
                             ring_hi[:, n % RING, 0:c], ring_lo[:, n % RING, 0:c], k == 0, k == NK - 1)

            def unit(u):
                b, t = u // NT, u % NT
                if u < NT + 2:
                    pe.wait_ge(taken, u - NT + 1)
                elif u - 2 < N_ACT_UNITS:
                    pe.wait_ge(taken, u - 1)
                else:
                    pe.wait_ge(res_done, u - 2 - OUT0 + 1)
                for k in range(NK):
                    n = b * NK + k
                    if t == 0:
                        pe.wait_ge(w_lo, n + 1)
                    last = product(u, k, bank(u % 2), n)
                    if t == NT - 1 and k < NK - 1:
                        last.then_inc(w_used, 1)
                last.then_inc(dense, 1)

            for k in range(NK):
                pe.wait_ge(x_lo, k + 1)
                pe.wait_ge(w_lo, k + 1)
                for t in range(NT):
                    last = product(t, k, bank(t), k)
                    if k == NK - 1:
                        last.then_inc(dense, 1)
                if k < NK - 1:
                    last.then_inc(w_used, 1)
            for b in ("v", "akv"):
                for t in range(NT):
                    unit(first_unit[b] + t)

            def transpose(dst, src):
                return nc.tensor.transpose(dst, src, ident)

            def ret_transpose(t):
                pe.wait_ge(rot_s, t + 1)
                if t:
                    pe.wait_ge(rT_out, t)
                for j in range(4):
                    last = transpose(bank(4)[:, tok(j)], rqk[:, t, tok(j)])
                last.then_inc(rT, 1)

            def ak_transpose(t):
                pe.wait_ge(arotk_s, t + 1)
                if t:
                    pe.wait_ge(akT_out, t)
                transpose(bank(3)[:, 0:P], akv[:, t, 0:P]).then_inc(akT, 1)

            def ret_scores(t):
                pe.wait_ge(rT_out, t + 1)
                if t:
                    pe.wait_ge(r_decayed, t)
                for p in range(2):
                    last = mm(bank(5)[:, p * 256:(p + 1) * 256], kT_ret[:, p, :],
                              qT_ret[:, t % 2, p, :, :], start=True, stop=True)
                last.then_inc(r_score, 1)
                if t < NT - 1:
                    pe.wait_ge(kd_s, t + 1)
                    if t:
                        pe.wait_ge(r_state, t)
                    for p in range(2):
                        last = mm(bank(6)[:, p * 256:(p + 1) * 256], kdec[:, tok(p)],
                                  rvy[:, t, p * 256:(p + 1) * 256], start=True, stop=True)
                    last.then_inc(r_kv, 1)

            def ret_output(t):
                pe.wait_ge(r_decayed, t + 1)
                if t:
                    pe.wait_ge(r_state, t)
                    pe.wait_ge(r_sq, t)
                for h in range(RET_HEADS):
                    p, s = divmod(h, 2)
                    last = mm(bank(7)[:, tok(h)], score[:, h, :], rvy[:, t, tok(h)], start=True, stop=t == 0)
                    if t:
                        last = mm(bank(7)[:, tok(h)], qT_ret[:, t % 2, p, s, :],
                                  state[:, t % 2, p, tok(s)], start=False, stop=True)
                last.then_inc(r_y, 1)

            def aq_transpose(t):
                pe.wait_ge(arotq_s, t + 1)
                if t:
                    pe.wait_ge(m_lo, t)
                for c in range(4):
                    last = transpose(bank(2)[:, tok(c)], aq[:, t % 2, tok(c)])
                last.then_inc(aqT, 1)

            def att_scores(t):
                pe.wait_ge(aqT_out, t + 1)
                if t:
                    pe.wait_ge(a_exp, 2 * t)
                else:
                    pe.wait_ge(akT_out, NT)
                    pe.wait_ge(r_decayed, NT)
                for e in range(2):
                    n = 2 * t + e
                    dst = bank(4 + e).rearrange("p (c g k) -> p c g k", c=2, g=KV_HEADS)
                    runs = [(0, n * CHUNK, CHUNK), (CHUNK, (n - 1) * CHUNK, CHUNK)] if e == 0 else \
                           [(0, (n - 1) * CHUNK, 2 * CHUNK)]
                    for cp in range(2):
                        for at_key, key, size in runs[:1] if n == 0 else runs:
                            last = mm(dst[:, cp, :, at_key:at_key + size],
                                      qT_att[:, e, 2 * cp:2 * cp + 2, :].rearrange("p c i -> p (c i)"),
                                      kT_att[:, :, key:key + size], start=True, stop=True)
                    last.then_inc(a_score, 1)

            def probs_transpose(t):
                for e in range(2):
                    pe.wait_ge(a_prob, 2 * t + e + 1)
                    if t:
                        pe.wait_ge(a_pT_out, 2 * t - 1 + e)
                    elif e:
                        pe.wait_ge(r_sq, NT)
                    else:
                        pe.wait_ge(r_state, NT - 1)
                    for b in range(4):
                        last = transpose(bank(6 + e)[:, tok(b)], probs[:, e, b, :])
                    last.then_inc(a_pT, 1)

            def att_output(t):
                pe.wait_ge(a_pT_out, 2 * t + 2)
                pe.wait_ge(veven_s, 2 * t + 1)
                if t:
                    pe.wait_ge(a_lo, t)
                for e in range(2):
                    pt = probsT[:, e, :, :].rearrange("p (c g) q -> p c g q", c=2)
                    for g in range(KV_HEADS):
                        v = akv[:, t, P + g * HEAD:P + (g + 1) * HEAD] if e else \
                            v_even[:, t, g * HEAD:(g + 1) * HEAD]
                        last = mm(bank(3)[g * HEAD:(g + 1) * HEAD, e * 256:(e + 1) * 256], v, pt[:, :, g, :],
                                  start=True, stop=True)
                last.then_inc(a_y, 1)

            def mix_transpose(t):
                pe.wait_ge(r_gated, t + 1)
                pe.wait_ge(aqT_out, t + 1)
                for h in range(RET_HEADS):
                    last = transpose(bank(2)[:, tok(h)], rvy[:, t, tok(h)])
                last.then_inc(m_T, 1)

            for t in range(NT):
                ret_transpose(t)
                ak_transpose(t)
                unit(first_unit["gate"] + t)
                ret_scores(t)
                if t:
                    ret_output(t - 1)
            for s in range(NT + 3):
                if 1 <= s <= NT:
                    aq_transpose(s - 1)
                if s >= NT:
                    pe.wait_ge(m_lo, s - NT + 1)
                    pe.wait_ge(a_lo, s - NT + 1)
                unit(first_unit["aq"] + s)
                if s == 0:
                    ret_output(NT - 1)
                if s >= 3:
                    att_output(s - 3)
                if 1 <= s <= NT:
                    mix_transpose(s - 1)
                if 2 <= s <= NT + 1:
                    probs_transpose(s - 2)
                if 1 <= s <= NT:
                    att_scores(s - 1)
            for t in range(3, NT):
                pe.wait_ge(m_lo, t + 1)
                pe.wait_ge(a_lo, t + 1)
                unit(OUT0 + t)

            def norm_transpose(n):
                t, pair = n % NT, psum[2 + n % 2]
                pe.wait_ge(n_h, n + 1)
                if n >= 2:
                    pe.wait_ge(n_lo, n - 1)
                elif n == 0:
                    pe.wait_ge(a_exp, 2 * NT)
                else:
                    pe.wait_ge(a_pT_out, 2 * NT)
                for k in range(NK):
                    last = transpose(pair[:, tok(k)], res[:, k // 4, t, tok(k % 4)])
                last.then_inc(n_T, 1)

            for t in range(NT):
                unit(OUT1 + t)
                if t >= 2:
                    norm_transpose(t - 2)

            def up_half(f, part, half):
                w_h, w_l = up_hi_t[f], up_lo_t[f]
                dst = psum[part][:, half * W:(half + 1) * W]
                cols, toks = slice(part * P, (part + 1) * P), slice(half * W, (half + 1) * W)
                for k in range(NK):
                    last = three(dst, w_h[:, k, cols], w_l[:, k, cols], actT_hi[:, k, toks],
                                 actT_lo[:, k, toks], k == 0, k == NK - 1)
                return last

            def up(f, i):
                pe.wait_ge(up_lo_s, i * 2 + (f + 1))
                for part in range(2):
                    pe.wait_ge(c_done, i * 4 + (2 * f + part - 1))
                    for half in range(2):
                        last = up_half(f, part, half)
                    last.then_inc(u_done, 1)

            pe.wait_ge(up_lo_s, 1)
            pe.wait_ge(n_lo, 4)
            pe.wait_ge(res_done, 2 * NT)
            up_half(0, 0, 0)
            norm_transpose(NT - 2)
            up_half(0, 1, 0)
            norm_transpose(NT - 1)
            pe.wait_ge(n_lo, NT)
            up_half(0, 0, 1).then_inc(u_done, 1)
            up_half(0, 1, 1).then_inc(u_done, 1)
            pe.wait_ge(up_lo_s, 2)
            for part in range(2):
                pe.wait_ge(c_done, part + 1)
                for half in range(2):
                    last = up_half(1, part, half)
                last.then_inc(u_done, 1)

            def down_units(i, first):
                pe.wait_ge(g_lo, i * 2 + 2)
                pe.wait_ge(dn_lo_s, i * 2 + 2)
                for t in range(NT):
                    if t > 1 or not first:
                        pe.wait_ge(d_added, i * NT + (t - 1))
                    for half in range(2):
                        dst = psum[2 + t % 2][:, half * W:(half + 1) * W]
                        for f in range(2):
                            last = three(dst, gT_hi[:, f, tok(t)], gT_lo[:, f, tok(t)],
                                         down_hi[:, f, half * W:(half + 1) * W],
                                         down_lo[:, f, half * W:(half + 1) * W], f == 0, f == 1)
                    last.then_inc(d_done, 1)

            up(0, 1)
            down_units(0, True)
            up(1, 1)
            with pe.Fori(2, PAIRS) as i:
                up(0, i)
                down_units(i - 1, False)
                up(1, i)
            down_units(PAIRS - 1, False)

            pe.wait_ge(pl_lo, 4)
            pe.wait_ge(c_done, 4 * PAIRS)
            for u in range(2 * NT):
                h, t = divmod(u, NT)
                if u >= 2:
                    pe.wait_ge(gt_mul, u - 1)
                for k in range(2):
                    last = three(bank(2 + u % 2), pT_hi[:, k, tok(t)], pT_lo[:, k, tok(t)],
                                 ple_hi[:, k, h * W:(h + 1) * W], ple_lo[:, k, h * W:(h + 1) * W],
                                 k == 0, k == 1)
                last.then_inc(pl_done, 1)
                if h == 0:
                    if t == 0:
                        pe.wait_ge(d_added, NT * PAIRS)
                    norm_transpose(NT + t)
                    pe.wait_ge(n_lo, NT + t + 1)
                if u >= 2:
                    pe.wait_ge(sig_s, u - 1)
                for k in range(NK):
                    n = h * NK + k
                    if t == 0:
                        pe.wait_ge(gw_lo, n + 1)
                    last = three(bank(u % 2), actT_hi[:, k, tok(t)], actT_lo[:, k, tok(t)],
                                 gw_hi_t[k // 4][:, k % 4, :], gw_lo_t[k // 4][:, k % 4, :],
                                 k == 0, k == NK - 1)
                    if t == NT - 1 and k < NK - 1:
                        last.then_inc(gw_used, 1)
                last.then_inc(gt_done, 1)

        @block.scalar
        def _(act):
            A = nc.scalar.activation

            def copy(dst, src):
                return A(dst, src, ACT.Copy)

            def used(n):
                b, k = divmod(n, NK)
                if k < NK - 1:
                    act.wait_ge(w_used, b * (NK - 1) + k + 1)
                else:
                    act.wait_ge(dense, (b + 1) * NT)

            def weight_hi(n):
                c = COLS[items[n][0]]
                act.wait_ge(w_in_s[n % RAWS], 16 * (n // RAWS + 1))
                if n >= RING:
                    used(n - RING)
                copy(ring_hi[:, n % RING, 0:c], w_raw[:, n % RAWS, 0:c]).then_inc(w_hi, 1)

            def next_weights(b, t):
                if b + 1 < len(BLOCKS):
                    for k in range(4, NK) if t == NT - 1 else [t - 1] if 1 <= t <= 4 else []:
                        weight_hi((b + 1) * NK + k)

            def take(u, dst, func=ACT.Copy):
                act.wait_ge(dense, u + 1)
                c = COLS[items[u][0]]
                A(dst, bank(u if u < NT else u % 2)[:, 0:c], func).then_inc(taken, 1)

            for k in range(NK):
                act.wait_ge(xT_in[k], 16)
                copy(actT_hi[:, k, :], xT_raw[:, k, :]).then_inc(x_hi, 1)
                weight_hi(k)
            for n in range(NK, 2 * NK):
                weight_hi(n)
            for t in range(NT):
                take(t, rqk[:, t, :])
            act.wait_ge(angle_s, 1)
            A(trig[:, 1, :, :], trig[:, 1, :, :], ACT.Sin).then_inc(sine_s, 1)
            A(trig[:, 0, :, :], trig[:, 0, :, :], ACT.Sin, scale=0.5).then_inc(sine_s, 1)
            for t in range(NT):
                take(NT + t, rvy[:, t, :])
                next_weights(1, t)
            for t in range(NT):
                take(2 * NT + t, akv[:, t, :])
                next_weights(2, t)

            def ret_transposed(t):
                act.wait_ge(rT, t + 1)
                if t:
                    act.wait_ge(r_score, t)
                if t >= 2:
                    act.wait_ge(r_y, t - 1)
                if t == 0:
                    act.wait_ge(zero_s, 2)
                b4 = bank(4).rearrange("p (a j q) -> p a j q", a=2, j=2)
                copy(kT_ret[:, :, :], b4[:, 1, :, :])
                for s in range(2):
                    rows = slice(s * 64, (s + 1) * 64)
                    last = copy(qT_ret[rows, t % 2, :, s, :], b4[rows, 0, :, :])
                last.then_inc(rT_out, 1)

            def ret_out(t):
                act.wait_ge(r_y, t + 1)
                copy(rvy[:, t, :], bank(7)).then_inc(r_yout, 1)
                if t:
                    act.wait_ge(r_ms, t)
                A(square[:, :], bank(7), ACT.Square).then_inc(r_sq, 1)

            for t in range(NT):
                ret_transposed(t)
                if t >= 2:
                    act.wait_ge(r_gated, t - 1)
                take(3 * NT + t, stage[:, t % 2, :], ACT.Silu)
                next_weights(3, t)
                if t:
                    ret_out(t - 1)

            def aq_transposed(t):
                act.wait_ge(aqT, t + 1)
                act.wait_ge(a_score, 2 * t) if t else act.wait_ge(r_ms, NT)
                copy(qT_att[:, :, :, :].rearrange("p e c i -> p c e i"),
                     bank(2).rearrange("p (c e i) -> p c e i", c=4, e=2)).then_inc(aqT_out, 1)

            def att_hi(t):
                act.wait_ge(a_y, t + 1)
                for e in range(2):
                    last = copy(actT_hi[:, 4:8, t * P + e * CHUNK:t * P + (e + 1) * CHUNK],
                                bank(3)[:, e * 256:(e + 1) * 256].rearrange("p (c i) -> p c i", c=4))
                last.then_inc(a_hi, 1)

            def mix_hi(t):
                act.wait_ge(m_T, t + 1)
                copy(actT_hi[:, 0:4, tok(t)], bank(2).rearrange("p (h q) -> p h q", h=4)).then_inc(m_hi, 1)

            def probs_transposed(t):
                for e in range(2):
                    act.wait_ge(a_pT, 2 * t + e + 1)
                    if t:
                        act.wait_ge(a_y, t)
                    copy(probsT[:, e, :, :], bank(6 + e)).then_inc(a_pT_out, 1)

            def exps(t):
                for e in range(2):
                    n = 2 * t + e
                    keys = CHUNK if n == 0 else 2 * CHUNK
                    act.wait_ge(a_max, n + 1)
                    if n == 0:
                        act.wait_ge(zero_s, 4)
                    if t:
                        act.wait_ge(a_pT, 2 * (t - 1) + e + 1)
                    dst = bank(4 + e).rearrange("p (b k) -> p b k", b=4)
                    for b in range(4):
                        A(probs[:, e, b, 0:keys], dst[:, b, 0:keys], ACT.Exp, bias=sneg[:, e, b:b + 1],
                          scale=HEAD ** -0.5, accum_out=ssum[:, e, b:b + 1])
                    A(sinke[:, e, :], sinkd[:, e, :], ACT.Exp).then_inc(a_exp, 1)

            for s in range(NT + 3):
                if 1 <= s <= NT:
                    aq_transposed(s - 1)
                if s < NT:
                    if s >= 2:
                        act.wait_ge(aqT, s - 1)
                    take(4 * NT + s, aq[:, s % 2, :])
                    next_weights(4, s)
                else:
                    next_weights(5, s - NT)
                if s == 0:
                    ret_out(NT - 1)
                if s >= 3:
                    att_hi(s - 3)
                if 1 <= s <= NT:
                    mix_hi(s - 1)
                if 2 <= s <= NT + 1:
                    probs_transposed(s - 2)
                if 1 <= s <= NT:
                    exps(s - 1)
            for t in range(3, NT):
                next_weights(5, t)

            def norm_z(n):
                t = n % NT
                act.wait_ge(n_bias, n + 1)
                r = res[:, :, t, :]
                A(r, r, ACT.Identity, bias=nbias[:, t:t + 1], scale=rstd[:, t:t + 1]).then_inc(n_z, 1)

            def norm_hi(n):
                act.wait_ge(n_T, n + 1)
                copy(actT_hi[:, :, tok(n % NT)], psum[2 + n % 2][:, :].rearrange("p (k q) -> p k q", k=NK))\
                    .then_inc(n_hi, 1)

            def residual_scaled(n):
                r = res[:, :, n % NT, :]
                A(r, r, ACT.Copy, scale=ALPHA).then_inc(n_alpha, 1)

            def up_split_hi(f, i):
                act.wait_ge(up_in[f], i * 16 + 16)
                act.wait_ge(u_done, i * 4 + (2 * f - 2)) if not isinstance(i, int) or i else None
                copy(up_hi_t[f][:, :, :], up_raw[:, f, :].rearrange("p (k n) -> p k n", k=NK)).then_inc(up_hi_s, 1)

            for t in range(NT + 1):
                if t:
                    norm_z(t - 1)
                if t >= 2 and t < NT:
                    norm_hi(t - 2)
                    residual_scaled(t - 2)
                if t == 3:
                    act.wait_ge(dense, (len(BLOCKS) - 1) * NT)
                    up_split_hi(0, 0)
                if t == 5:
                    up_split_hi(1, 0)
            for n in (NT - 2, NT - 1):
                norm_hi(n)
                residual_scaled(n)

            def conv_first(f, i):
                for part in range(2):
                    act.wait_ge(u_done, i * 4 + (2 * f + part + 1))
                    if not (isinstance(i, int) and i == 0 and f == 0):
                        act.wait_ge(g_lo, i * 2 + f)
                    par = convp[:, bass.ds(i * 2 + f, 1), part * 4:part * 4 + 4].rearrange("p o n -> p (o n)")
                    A(conv_ab[:, part, :], psum[part][:, :], ACT.Identity, scale=par[:, 2:3], bias=par[:, 3:4])\
                        .then_inc(c_init, 1)

            def gelu(f, i):
                act.wait_ge(c_done, i * 4 + (2 * f + 1))
                A(conv_ab[:, 0, :], conv_ab[:, 0, :], ACT.Gelu_apprx_tanh).then_inc(gelu_s, 1)

            def gated_hi(f, i):
                act.wait_ge(g_mul, i * 2 + (f + 1))
                if not (isinstance(i, int) and i == 0):
                    act.wait_ge(d_done, i * NT)
                copy(gT_hi[:, f, :], conv_ab[:, 0, :]).then_inc(g_hi, 1)

            def down_split_hi(f, i):
                act.wait_ge(down_in[f], i * 16 + 16)
                copy(down_hi[:, f, :], down_raw[:, f, :]).then_inc(dn_hi_s, 1)

            def turn(i, last):
                conv_first(0, i)
                gelu(0, i)
                if not last:
                    up_split_hi(0, i + 1)
                gated_hi(0, i)
                for f in range(2):
                    down_split_hi(f, i)
                conv_first(1, i)
                gelu(1, i)
                if not last:
                    up_split_hi(1, i + 1)
                gated_hi(1, i)

            act.wait_ge(conv_in_s, 16)
            act.wait_ge(dense, len(BLOCKS) * NT)
            turn(0, False)
            with act.Fori(1, PAIRS - 1) as i:
                turn(i, False)
            turn(PAIRS - 1, True)

            def gate_hi(n):
                k = n % NK
                act.wait_ge(gate_in[k], 16 * (n // NK + 1))
                if n >= NK:
                    act.wait_ge(gw_used, k + 1) if k < NK - 1 else act.wait_ge(gt_done, NT)
                elif k == 0 or k == 4:
                    act.wait_ge(u_done, 4 * PAIRS)
                copy(gw_hi_t[k // 4][:, k % 4, :], gate_raw[:, k, :]).then_inc(gw_hi, 1)

            for k in range(NK):
                gate_hi(k)
            act.wait_ge(ple_in, 64)
            act.wait_ge(d_done, NT * PAIRS)
            for k in range(2):
                copy(pT_hi[:, k, :], pT_raw[:, k, :]).then_inc(pl_hi, 1)
                copy(ple_hi[:, k, :], ple_raw[:, k, :]).then_inc(pl_hi, 1)
            norm_z(NT)
            norm_z(NT + 1)
            for u in range(2 * NT):
                h, t = divmod(u, NT)
                if h == 0:
                    norm_hi(NT + t)
                    if t + 2 < NT:
                        norm_z(NT + t + 2)
                    if t == NT - 1:
                        for k in range(NK):
                            gate_hi(NK + k)
                act.wait_ge(gt_done, u + 1)
                if u >= 2:
                    act.wait_ge(gt_mul, u - 1)
                else:
                    act.wait_ge(pl_lo, 4)
                A(sig[:, u % 2, :], bank(u % 2), ACT.Sigmoid).then_inc(sig_s, 1)

        @block.vector
        def _(dve):
            V = nc.vector
            steps = {"n": 0, "loop": None}

            def own(ins):
                ins.then_inc(dve_s, 1)
                steps["n"] += 1

            def settle():
                n = steps["n"]
                dve.wait_ge(dve_s, n if steps["loop"] is None else steps["loop"] + n)

            def subtract_lo(dst, src, hi):
                return V.tensor_tensor(dst, src, f32(hi), ALU.subtract)

            def weight_lo(n):
                c = COLS[items[n][0]]
                dve.wait_ge(w_hi, n + 1)
                subtract_lo(ring_lo[:, n % RING, 0:c], w_raw[:, n % RAWS, 0:c], ring_hi[:, n % RING, 0:c])\
                    .then_inc(w_lo, 1)

            def next_weights(b, t):
                if b + 1 < len(BLOCKS):
                    for k in range(4, NK) if t == NT - 1 else [t - 1] if 1 <= t <= 4 else []:
                        weight_lo((b + 1) * NK + k)

            for k in range(NK):
                dve.wait_ge(x_hi, k + 1)
                subtract_lo(actT_lo[:, k, :], xT_raw[:, k, :], actT_hi[:, k, :]).then_inc(x_lo, 1)
                weight_lo(k)
            for n in range(NK, 2 * NK):
                weight_lo(n)

            dve.wait_ge(cst_in_s, 16)
            dve.wait_ge(pos_in_s, 32)
            n_all = NT * NFREQ
            tmp = rot[:, :, 0:n_all].rearrange("p a (t f) -> p a t f", t=NT)
            ang, n_lo_t, n_hi_t = trig[:, 1, :, :], tmp[:, 0], tmp[:, 1]
            own(V.tensor_copy(posf, posi.bitcast(mybir.dt.int32)))
            settle()
            own(V.tensor_tensor(ang, posf.unsqueeze(2).to_broadcast([P, NT, NFREQ]),
                                freq.unsqueeze(1).to_broadcast([P, NT, NFREQ]), ALU.mult))
            settle()
            own(V.tensor_scalar(n_lo_t, ang, 1.0 / (2 * np.pi), ANGLE_MAGIC, ALU.mult, ALU.add))
            settle()
            own(V.tensor_scalar(n_lo_t, n_lo_t, ANGLE_MAGIC, None, ALU.subtract))
            settle()
            own(V.tensor_scalar(n_hi_t, n_lo_t, 2.0 ** -11, ANGLE_MAGIC, ALU.mult, ALU.add))
            settle()
            own(V.tensor_scalar(n_hi_t, n_hi_t, ANGLE_MAGIC, 2.0 ** 11, ALU.subtract, ALU.mult))
            settle()
            own(V.tensor_tensor(n_lo_t, n_lo_t, n_hi_t, ALU.subtract))
            settle()
            for part in TWO_PI:
                for n_part in (n_hi_t, n_lo_t):
                    own(V.scalar_tensor_tensor(out=ang, in0=n_part, scalar=-part, in1=ang, op0=ALU.mult, op1=ALU.add))
                    settle()
            own(V.tensor_scalar(ang, ang, PI_BELOW, -PI_BELOW, ALU.min, ALU.max))
            settle()
            V.tensor_copy(trig[:, 0, :, :], ang).then_inc(angle_s, 1)
            dve.wait_ge(sine_s, 2)
            cosines = trig[:, 0, :, :]
            own(V.tensor_tensor(cosines, cosines, cosines, ALU.mult))
            settle()
            own(V.tensor_scalar(cosines, cosines, -2.0, 1.0, ALU.mult, ALU.add))
            settle()

            def rotary(view, cos, sin, buf, heads, half):
                shape = [P, heads, 2, half]
                c = cos.unsqueeze(1).unsqueeze(1).to_broadcast(shape)
                s = sin.unsqueeze(1).unsqueeze(1).to_broadcast(shape)
                by_cos = buf[:, 0, 0:heads * 2 * half].rearrange("p (n a h) -> p n a h", n=heads, a=2)
                by_sin = buf[:, 1, 0:heads * 2 * half].rearrange("p (n a h) -> p n a h", n=heads, a=2)
                own(V.tensor_tensor(by_cos, view, c, ALU.mult))
                own(V.tensor_tensor(by_sin, view, s, ALU.mult))
                settle()
                own(V.tensor_tensor(view[:, :, 0, :], by_cos[:, :, 0, :], by_sin[:, :, 1, :], ALU.subtract))
                last = V.tensor_tensor(view[:, :, 1, :], by_cos[:, :, 1, :], by_sin[:, :, 0, :], ALU.add)
                return last

            def ret_rotary(t):
                dve.wait_ge(taken, t + 1)
                if t:
                    dve.wait_ge(rot_s, t)
                view = rqk[:, t, :].rearrange("p (n a h) -> p n a h", n=2 * RET_HEADS, a=2)
                own(rotary(view, cos_r[:, t, :], sin_r[:, t, :], rot, 2 * RET_HEADS, HALF_R))
                settle()
                q = rqk[:, t, 0:256].rearrange("p (h d) -> p h d", h=RET_HEADS)
                V.tensor_tensor(q, q, q_decay.unsqueeze(2).to_broadcast([P, RET_HEADS, RET_QK]), ALU.mult)\
                    .then_inc(rot_s, 1)

            for t in range(NT):
                ret_rotary(t)
                next_weights(1, t)
            for t in range(NT):
                dve.wait_ge(taken, 2 * NT + t + 1)
                if t:
                    dve.wait_ge(arotk_s, t)
                view = akv[:, t, 0:P].rearrange("p (n d) -> p n d", n=KV_HEADS)[:, :, 0:ROPE_DIM]\
                    .rearrange("p n (a h) -> p n a h", a=2)
                rotary(view, cos_a[:, t, :], sin_a[:, t, :], arot, KV_HEADS, HALF_A).then_inc(arotk_s, 1)
                next_weights(2, t)

            def ret_gate(t):
                dve.wait_ge(r_rms, t + 1)
                dve.wait_ge(taken, 3 * NT + t + 1)
                for h in range(RET_HEADS):
                    y = rvy[:, t, tok(h)]
                    last = V.scalar_tensor_tensor(out=y, in0=y, scalar=rms[:, t % 2, h:h + 1],
                                                  in1=stage[:, t % 2, tok(h)], op0=ALU.mult, op1=ALU.mult)
                last.then_inc(r_gated, 1)

            def ret_square_sum(t):
                dve.wait_ge(r_sq, t + 1)
                if t >= 2:
                    dve.wait_ge(r_rms, t - 1)
                own(V.reduce_sum(rsum[:, t % 2, :], square[:, :].rearrange("p (h e) -> p h e", h=RET_HEADS), AX.X))
                settle()
                V.tensor_scalar(rsum[:, t % 2, :], rsum[:, t % 2, :], 1.0 / RET_V, RMS_EPS, ALU.mult, ALU.add)\
                    .then_inc(r_ms, 1)

            for t in range(NT):
                if t >= 2:
                    ret_gate(t - 2)
                if t < NT - 1:
                    if t:
                        dve.wait_ge(r_kv, t)
                    dve.wait_ge(rot_s, t + 1)
                    k = rqk[:, t, 256:512].rearrange("p (h d) -> p h d", h=RET_HEADS)
                    V.tensor_tensor(kdec[:, :].rearrange("p (h d) -> p h d", h=RET_HEADS), k,
                                    k_decay.unsqueeze(2).to_broadcast([P, RET_HEADS, RET_QK]), ALU.mult)\
                        .then_inc(kd_s, 1)
                dve.wait_ge(akT, t + 1)
                if t == 0:
                    dve.wait_ge(zero_s, 2)
                for g in range(KV_HEADS):
                    rows = slice(g * HEAD, (g + 1) * HEAD)
                    last = V.tensor_copy(kT_att[rows, g, tok(t)], bank(3)[rows, 0:P])
                last.then_inc(akT_out, 1)
                next_weights(3, t)
                dve.wait_ge(r_score, t + 1)
                if t:
                    dve.wait_ge(r_y, t)
                V.tensor_tensor(score[:, :, :], bank(5).rearrange("p (h q) -> p h q", h=RET_HEADS), decayT, ALU.mult)\
                    .then_inc(r_decayed, 1)
                if t < NT - 1:
                    dve.wait_ge(r_kv, t + 1)
                    for p in range(2):
                        dst, kv = state[:, (t + 1) % 2, p, :], bank(6)[:, p * 256:(p + 1) * 256]
                        if t == 0:
                            last = V.tensor_copy(dst, kv)
                        else:
                            if p == 0:
                                dve.wait_ge(r_state, t)
                            last = V.scalar_tensor_tensor(out=dst, in0=state[:, t % 2, p, :],
                                                          scalar=state_decay[:, p:p + 1], in1=kv,
                                                          op0=ALU.mult, op1=ALU.add)
                    last.then_inc(r_state, 1)
                if t:
                    ret_square_sum(t - 1)

            def att_max(t):
                for e in range(2):
                    n = 2 * t + e
                    keys = CHUNK if n == 0 else 2 * CHUNK
                    dve.wait_ge(a_score, n + 1)
                    s = bank(4 + e).rearrange("p (b k) -> p b k", b=4)[:, :, 0:keys]
                    own(V.reduce_max(smax[:, e, :], s, AX.X))
                    settle()
                    own(V.scalar_tensor_tensor(out=smax[:, e, :], in0=smax[:, e, :], scalar=HEAD ** -0.5,
                                               in1=sink, op0=ALU.mult, op1=ALU.max))
                    settle()
                    own(V.tensor_tensor(sinkd[:, e, :], sink, smax[:, e, :], ALU.subtract))
                    V.tensor_scalar(sneg[:, e, :], smax[:, e, :], -1.0, None, ALU.mult).then_inc(a_max, 1)

            def att_normalise(t):
                for e in range(2):
                    dve.wait_ge(a_exp, 2 * t + e + 1)
                    own(V.tensor_tensor(srec[:, e, :], ssum[:, e, :], sinke[:, e, :], ALU.add))
                    settle()
                    own(V.reciprocal(srec[:, e, :], srec[:, e, :]))
                    settle()
                    V.tensor_tensor(probs[:, e, :, :], probs[:, e, :, :],
                                    srec[:, e, :].unsqueeze(2).to_broadcast([P, 4, P]), ALU.mult).then_inc(a_prob, 1)

            def residual_add(u):
                h, t = divmod(u, NT)
                dve.wait_ge(dense, OUT0 + u + 1)
                dve.wait_ge(xres_in[u % 2], 16 * (u // 2 + 1))
                V.scalar_tensor_tensor(out=res[:, h, t, :], in0=stage[:, u % 2, :], scalar=ALPHA,
                                       in1=bank(u % 2), op0=ALU.mult, op1=ALU.add).then_inc(res_done, 1)

            for s in range(NT + 3):
                if s == 0:
                    ret_gate(NT - 2)
                    ret_square_sum(NT - 1)
                if s == 1:
                    ret_gate(NT - 1)
                if s < NT:
                    dve.wait_ge(taken, 4 * NT + s + 1)
                    dve.wait_ge(arotq_s, s) if s else dve.wait_ge(arotk_s, NT)
                    view = aq[:, s % 2, :].rearrange("p (n d) -> p n d", n=Q_HEADS)[:, :, 0:ROPE_DIM]\
                        .rearrange("p n (a h) -> p n a h", a=2)
                    rotary(view, cos_a[:, s, :], sin_a[:, s, :], arot, Q_HEADS, HALF_A).then_inc(arotq_s, 1)
                    next_weights(4, s)
                else:
                    residual_add(s - NT)
                    next_weights(5, s - NT)
                if s >= 3:
                    t = s - 3
                    dve.wait_ge(a_hi, t + 1)
                    for e in range(2):
                        cols = slice(t * P + e * CHUNK, t * P + (e + 1) * CHUNK)
                        last = subtract_lo(actT_lo[:, 4:8, cols],
                                           bank(3)[:, e * 256:(e + 1) * 256].rearrange("p (c i) -> p c i", c=4),
                                           actT_hi[:, 4:8, cols])
                    last.then_inc(a_lo, 1)
                if 1 <= s <= NT:
                    t = s - 1
                    dve.wait_ge(m_hi, t + 1)
                    subtract_lo(actT_lo[:, 0:4, tok(t)], bank(2).rearrange("p (h q) -> p h q", h=4),
                                actT_hi[:, 0:4, tok(t)]).then_inc(m_lo, 1)
                    att_max(t)
                    att_normalise(t)
            for t in range(3, NT):
                residual_add(t)
                next_weights(5, t)

            def norm_stats(n):
                t, s = n % NT, n % 2
                for h in range(2):
                    own(V.bn_stats(bnst[:, s, 6 * h:6 * h + 6], res[:, h, t, :]))
                settle()
                own(V.bn_aggr(mean[:, t, :], bnst[:, s, :]))
                settle()
                V.tensor_scalar(vare[:, t:t + 1], mean[:, t, 1:2], LN_EPS, None, ALU.add).then_inc(n_var, 1)

            def norm_bias(n):
                t = n % NT
                dve.wait_ge(n_rstd, n + 1)
                V.tensor_scalar(nbias[:, t:t + 1], mean[:, t, 0:1], rstd[:, t:t + 1], -1.0, ALU.mult, ALU.mult)\
                    .then_inc(n_bias, 1)

            def norm_gain(n):
                dve.wait_ge(n_z, n + 1)
                dve.wait_ge(gains_in, 32 if n < NT else 64)
                r = res[:, :, n % NT, :]
                V.tensor_tensor(r, r, gains[:, 0, :, :], ALU.mult).then_inc(n_gain, 1)

            def norm_lo(n):
                dve.wait_ge(n_hi, n + 1)
                subtract_lo(actT_lo[:, :, tok(n % NT)], psum[2 + n % 2][:, :].rearrange("p (k q) -> p k q", k=NK),
                            actT_hi[:, :, tok(n % NT)]).then_inc(n_lo, 1)

            def up_split_lo(f, i):
                dve.wait_ge(up_hi_s, i * 2 + (f + 1))
                subtract_lo(up_lo_t[f][:, :, :], up_raw[:, f, :].rearrange("p (k n) -> p k n", k=NK),
                            up_hi_t[f][:, :, :]).then_inc(up_lo_s, 1)

            for t in range(NT + 1):
                if t:
                    norm_bias(t - 1)
                if t < NT:
                    residual_add(NT + t)
                    dve.wait_ge(res_done, NT + t + 1)
                    norm_stats(t)
                if t:
                    norm_gain(t - 1)
                if 2 <= t < NT:
                    norm_lo(t - 2)
                if t == 3:
                    up_split_lo(0, 0)
                if t == 5:
                    up_split_lo(1, 0)
            for n in (NT - 2, NT - 1):
                norm_lo(n)

            def conv_taps(f, i):
                for part in range(2):
                    dve.wait_ge(c_init, i * 4 + (2 * f + part + 1))
                    par = convp[:, bass.ds(i * 2 + f, 1), part * 4:part * 4 + 4].rearrange("p o n -> p (o n)")
                    for back in (1, 2):
                        c, u = conv_ab[:, part, back:TOKENS], psum[part][:, 0:TOKENS - back]
                        ins = V.scalar_tensor_tensor(out=c, in0=u, scalar=par[:, 2 - back:3 - back], in1=c,
                                                     op0=ALU.mult, op1=ALU.add)
                        if back == 1:
                            own(ins)
                            settle()
                    ins.then_inc(c_done, 1)

            def gated(f, i):
                dve.wait_ge(gelu_s, i * 2 + (f + 1))
                dve.wait_ge(c_done, i * 4 + (2 * f + 2))
                V.tensor_tensor(conv_ab[:, 0, :], conv_ab[:, 0, :], conv_ab[:, 1, :], ALU.mult).then_inc(g_mul, 1)
                dve.wait_ge(g_hi, i * 2 + (f + 1))
                subtract_lo(gT_lo[:, f, :], conv_ab[:, 0, :], gT_hi[:, f, :]).then_inc(g_lo, 1)

            def down_split_lo(f, i):
                dve.wait_ge(dn_hi_s, i * 2 + (f + 1))
                subtract_lo(down_lo[:, f, :], down_raw[:, f, :], down_hi[:, f, :]).then_inc(dn_lo_s, 1)

            def down_add(i, t):
                dve.wait_ge(d_done, i * NT + (t + 1))
                r = res[:, :, t, :]
                V.tensor_tensor(r, r, psum[2 + t % 2][:, :].rearrange("p (h n) -> p h n", h=2), ALU.add)\
                    .then_inc(d_added, 1)

            def turn(i, first, last):
                conv_taps(0, i)
                if not first:
                    for t in range(NT):
                        down_add(i - 1, t)
                if not last:
                    up_split_lo(0, i + 1)
                gated(0, i)
                for f in range(2):
                    down_split_lo(f, i)
                conv_taps(1, i)
                if not last:
                    up_split_lo(1, i + 1)
                gated(1, i)

            dve.wait_ge(n_alpha, NT)
            turn(0, True, False)
            own_per_turn, before = 4, steps["n"]
            with dve.Fori(1, PAIRS - 1) as i:
                steps["loop"], steps["n"] = i * own_per_turn, before - own_per_turn
                turn(i, False, False)
            assert steps["n"] == before
            steps["loop"], steps["n"] = None, before + own_per_turn * (PAIRS - 2)
            turn(PAIRS - 1, False, True)

            def gate_lo(n):
                k = n % NK
                dve.wait_ge(gw_hi, n + 1)
                subtract_lo(gw_lo_t[k // 4][:, k % 4, :], gate_raw[:, k, :], gw_hi_t[k // 4][:, k % 4, :])\
                    .then_inc(gw_lo, 1)

            for k in range(NK):
                gate_lo(k)
            for t in range(NT):
                down_add(PAIRS - 1, t)
                if t < 2:
                    dve.wait_ge(d_added, (PAIRS - 1) * NT + t + 1)
                    norm_stats(NT + t)
            for k in range(2):
                dve.wait_ge(pl_hi, 2 * k + 1)
                subtract_lo(pT_lo[:, k, :], pT_raw[:, k, :], pT_hi[:, k, :]).then_inc(pl_lo, 1)
                dve.wait_ge(pl_hi, 2 * k + 2)
                subtract_lo(ple_lo[:, k, :], ple_raw[:, k, :], ple_hi[:, k, :]).then_inc(pl_lo, 1)
            norm_bias(NT)
            norm_bias(NT + 1)
            dve.wait_ge(d_added, PAIRS * NT)
            norm_stats(NT + 2)
            norm_gain(NT)
            norm_gain(NT + 1)
            for u in range(2 * NT):
                h, t = divmod(u, NT)
                if h == 0:
                    if t + 2 < NT:
                        norm_bias(NT + t + 2)
                    norm_lo(NT + t)
                    if t + 3 < NT:
                        norm_stats(NT + t + 3)
                    if t + 2 < NT:
                        norm_gain(NT + t + 2)
                    if t == NT - 1:
                        for k in range(NK):
                            gate_lo(NK + k)
                dve.wait_ge(pl_done, u + 1)
                dve.wait_ge(sig_s, u + 1)
                if u >= 2:
                    dve.wait_ge(out_s[u % 2], 16 * (u // 2))
                o = outs[:, u % 2, :]
                V.tensor_tensor(o, bank(2 + u % 2), sig[:, u % 2, :], ALU.mult).then_inc(gt_mul, 1)
                dve.wait_ge(gt_mul, u + 1)
                V.tensor_tensor(o, o, res[:, h, t, :], ALU.add).then_inc(gt_add, 1)

        @block.gpsimd
        def _(pool):
            G = nc.gpsimd
            G.memset(qT_ret[:, :, :, :, :], 0.0).then_inc(zero_s, 1)
            G.memset(kT_att[:, :, :], 0.0).then_inc(zero_s, 1)
            G.memset(v_even[:, 0, :], 0.0).then_inc(zero_s, 1)
            pool.wait_ge(zero_s, 3)
            for t in range(NT):
                pool.wait_ge(taken, 2 * NT + t + 1)
                own_rows, next_rows = slice(0, CHUNK), slice(CHUNK, P)
                G.tensor_copy(v_even[own_rows, t, :], akv[own_rows, t, P:2 * P]).then_inc(veven_s, 1)
                pool.wait_ge(veven_s, 2 * t + 1)
                if t < NT - 1:
                    G.tensor_copy(v_even[next_rows, t + 1, :], akv[next_rows, t, P:2 * P]).then_inc(veven_s, 1)
                    pool.wait_ge(veven_s, 2 * t + 2)
            for t in range(NT):
                pool.wait_ge(r_ms, t + 1)
                if t >= 2:
                    pool.wait_ge(r_gated, t - 1)
                G.tensor_tensor(rms[:, t % 2, :], rsum[:, t % 2, :], minus_half, ALU.pow).then_inc(r_rms, 1)
                if t == 1:
                    pool.wait_ge(rot_s, NT)
                    G.memset(probs[:, 0, :, CHUNK:P], 0.0).then_inc(zero_s, 1)

            def norm_add(n):
                pool.wait_ge(n_gain, n + 1)
                r = res[:, :, n % NT, :]
                G.tensor_tensor(r, r, gains[:, 1, :, :], ALU.add).then_inc(n_h, 1)

            for first in (0, NT):
                for n in range(first, first + NT):
                    t = n % NT
                    pool.wait_ge(n_var, n + 1)
                    G.tensor_tensor(rstd[:, t:t + 1], vare[:, t:t + 1], minus_half[:, 0:1], ALU.pow)\
                        .then_inc(n_rstd, 1)
                    if t:
                        norm_add(n - 1)
                norm_add(first + NT - 1)


def retention_constants():
    gamma = 1.0 - 2.0 ** (-5.0 - np.arange(RET_HEADS))
    i, j = np.arange(P)[None, :], np.arange(P)[:, None]
    same, later = i // CHUNK == j // CHUNK, i // CHUNK > j // CHUNK
    c = np.zeros((P, C_END), np.float64)
    scale = RET_QK ** -0.5
    for h, g in enumerate(gamma):
        d = np.where(same, g ** np.abs(i - j), np.where(later, g ** np.maximum(i - j, 0), 0.0))
        c[:, C_DECAY + h * P:C_DECAY + (h + 1) * P] = d * g ** -(i + 1.0) * scale
        c[:, C_QDEC + h] = g ** (np.arange(P) + 1.0)
        c[:, C_KDEC + h] = g ** (P - 1.0 - np.arange(P)) * scale
    for p in range(2):
        c[:64, C_SDEC + p], c[64:, C_SDEC + p] = gamma[2 * p] ** P, gamma[2 * p + 1] ** P
    c[:, C_IDENT:C_QDEC] = np.eye(P)
    c = c.astype(np.float32)
    ret = 10000.0 ** -(np.arange(HALF_R, dtype=np.float32) * np.float32(1 / (HALF_R - 1))).astype(np.float64)
    att = 500000.0 ** -(np.arange(HALF_A, dtype=np.float32) / HALF_A).astype(np.float64)
    c[:, C_FREQ:C_FREQ + HALF_R], c[:, C_FREQ + HALF_R:C_MHALF] = ret, att
    c[:, C_MHALF:C_END] = -0.5
    return c


def kernel(x, p, positions, w_in, w_out, attn_sinks, ln1_g, ln1_b, w_up, conv_w, conv_b,
           w_down, ln2_g, ln2_b, w_ple_gate, w_ple_proj):
    import concourse.bacc as bacc
    from concourse.bass_utils import run_bass_kernel_spmd

    a = np.ascontiguousarray
    x, p, w_in, w_out = np.asarray(x)[0], np.asarray(p)[0, 0], np.asarray(w_in)[0], np.asarray(w_out)[0]
    w_up, w_down = np.asarray(w_up)[0], np.asarray(w_down)[0]
    conv_w, conv_b = np.asarray(conv_w)[0], np.asarray(conv_b)[0]
    heads = np.arange(Q_HEADS * HEAD).reshape(KV_HEADS, 4, HEAD).transpose(1, 0, 2).reshape(-1)
    qk, v, g = np.arange(512), np.arange(512, 1024), np.arange(1024, 1536)
    aq, akv = 1536 + heads, np.arange(2048, 2304)
    w_in = w_in[:, np.concatenate([qk, v, akv, g, aq])]
    w_out = w_out[np.concatenate([np.arange(512), 512 + heads]), :]
    sinks = np.asarray(attn_sinks)[0].reshape(KV_HEADS, 2, 2)
    sinks = np.repeat(sinks.transpose(2, 1, 0).reshape(2, 4), CHUNK, axis=0)
    up = w_up.reshape(NK, P, 2, NF, P).transpose(3, 1, 0, 2, 4).reshape(NF, P, NK * 256)
    down = w_down.reshape(NF, P, MODEL)
    conv = np.concatenate([conv_w, conv_b[None]], 0).reshape(4, 2, NF, P).transpose(3, 2, 1, 0).reshape(P, NF, 8)
    ln = np.stack([np.asarray(t)[0] for t in (ln1_g, ln1_b, ln2_g, ln2_b)]).reshape(4, 2, W)
    ins = {
        "xT": x.T, "x": x, "pT": p.T, "pos": np.asarray(positions)[0].reshape(NT, P).T,
        "w_in": w_in, "w_out": w_out, "sinks": sinks, "ln": ln, "ff_up": up, "ff_down": down,
        "conv": conv, "w_gate": np.asarray(w_ple_gate)[0], "w_ple": np.asarray(w_ple_proj)[0],
        "cst_in": retention_constants(),
    }
    nc = bacc.Bacc("TRN2", target_bir_lowering=False, num_devices=1)
    arrays, args = {}, {}
    for name, t in ins.items():
        t = a(t)
        arrays[f"{name}_dram"] = t
        args[name] = nc.dram_tensor(f"{name}_dram", t.shape, mybir.dt.from_np(t.dtype), kind="ExternalInput").ap()
    args["out"] = nc.dram_tensor("out_dram", (TOKENS, MODEL), mybir.dt.float32, kind="ExternalOutput").ap()
    build(nc, **args)
    r = run_bass_kernel_spmd(nc, [arrays], core_ids=[0])
    return r.results[0]["out_dram"].reshape(1, TOKENS, MODEL)
```

```python
import numpy as np
import concourse.bass as bass
from concourse import mybir
from contextlib import ExitStack

P = 128
TOKENS = 1024
MODEL = 1024
NT = TOKENS // P
NK = MODEL // P
CHUNK = 64
RET_HEADS, RET_QK, RET_V = 4, 64, 128
Q_HEADS, KV_HEADS, HEAD = 8, 2, 64
PLE = 256
FF = 2816
NF = FF // P
PAIRS = NF // 2
ROPE_DIM = HEAD // 4
HALF_R, HALF_A = RET_QK // 2, ROPE_DIM // 2
NFREQ = HALF_R + HALF_A
ALPHA = 2.0 ** 0.25
LN_EPS, RMS_EPS = 1e-5, 1e-6
W = 512
ANGLE_MAGIC = 1.5 * 2.0 ** 23
TWO_PI = (6.28125, 1.9340515136718750e-3, 1.2551362e-6)
PI_BELOW = 3.1415925

C_DECAY, C_IDENT = 0, RET_HEADS * P
C_QDEC = C_IDENT + P
C_KDEC = C_QDEC + RET_HEADS
C_SDEC = C_KDEC + RET_HEADS
C_FREQ = C_SDEC + 2
C_MHALF = C_FREQ + NFREQ
C_END = C_MHALF + RET_HEADS

BLOCKS = ("qk", "v", "akv", "gate", "aq", "out0", "out1")
COLS = {"qk": 512, "v": 512, "akv": 256, "gate": 512, "aq": 512, "out0": 512, "out1": 512}
ALL, HALVES = (slice(0, TOKENS),), (slice(0, TOKENS // 2), slice(TOKENS // 2, TOKENS))
LAST_PAIRS = (3, 2, 0, 1, 3, 0, 1, 3)
GATE_LO_POOL = (NK - 2, NK - 1)
RING, RAWS = 12, 4


def build(nc, xT, x, pT, pos, w_in, w_out, sinks, ln, ff_up, ff_down, conv, w_gate, w_ple, cst_in, out):
    fp32, f32r = mybir.dt.float32, mybir.dt.float32r
    ALU, ACT, AX = mybir.AluOpType, mybir.ActivationFunctionType, mybir.AxisListType
    ctx = ExitStack()
    with ctx:
        base = nc.sbuf_base + (-nc.sbuf_base) % 64

        def at(name, offset, shape, dt=fp32):
            return nc.alloc_sbuf_tensor_at(name, [P] + list(shape), dt, offset=base + offset)

        KB = 1024
        actT_hi = at("actT_hi", 0, [NK, TOKENS], f32r)
        actT_lo = at("actT_lo", 32 * KB, [NK, TOKENS], f32r)
        RES = 64 * KB
        xT_raw = at("xT_raw", RES, [NK, TOKENS])
        rqk = at("rqk", RES, [NT, 512])
        rvy = at("rvy", RES + 16 * KB, [NT, 512])
        res = at("res", RES, [2, NT, W])
        RNG = 96 * KB
        ring_hi = at("ring_hi", RNG, [RING, W], f32r)
        ring_lo = at("ring_lo", RNG + 24 * KB, [RING, W], f32r)
        down_hi = at("down_hi", RNG, [2, MODEL], f32r)
        down_lo = at("down_lo", RNG + 24 * KB, [2, MODEL], f32r)
        gT_hi = at("gT_hi", RNG + 8 * KB, [2, TOKENS], f32r)
        gT_lo = at("gT_lo", RNG + 32 * KB, [2, TOKENS], f32r)
        up1_hi = at("up1_hi", RNG + 16 * KB, [NK, 256], f32r)
        up1_lo = at("up1_lo", RNG + 40 * KB, [NK, 256], f32r)
        pT_hi = at("pT_hi", RNG, [2, TOKENS], f32r)
        pT_lo = at("pT_lo", RNG + 24 * KB, [2, TOKENS], f32r)
        ple_hi = at("ple_hi", RNG + 8 * KB, [2, MODEL], f32r)
        ple_lo = at("ple_lo", RNG + 32 * KB, [2, MODEL], f32r)
        gw1_hi = at("gw1_hi", RNG + 16 * KB, [4, W], f32r)
        gw1_lo = at("gw1_lo", RNG + 40 * KB, [4, W], f32r)
        RAW = 144 * KB
        w_raw = at("w_raw", RAW, [RAWS, W])
        conv_ab = at("conv_ab", RAW, [2, TOKENS])
        pT_raw = at("pT_raw", RAW, [2, TOKENS])
        sig = at("sig", RAW, [2, W])
        outs = at("outs", RAW + 4 * KB, [2, W])
        M = 152 * KB
        cst = at("cst", M, [C_END])
        M += C_END * 4 + (-C_END * 4) % 64
        small = at("small", M, [256])
        M += 1024
        convp = at("convp", M, [NF, 8])
        M += NF * 32
        MIX = M
        sizes = {}

        def mix(name, shape, dt=fp32):
            sizes[name] = MIX + sizes.get("end", 0)
            t = at(name, sizes[name], shape, dt)
            sizes["end"] = sizes.get("end", 0) + int(np.prod(shape)) * 4
            return t

        kT_att = mix("kT_att", [KV_HEADS, TOKENS])
        akv = mix("akv", [NT, 256])
        v_even = mix("v_even", [NT, P])
        trig = mix("trig", [2, NT, NFREQ])
        probs = mix("probs", [2, 4, P])
        rot = at("rot", sizes["probs"], [2, 512])
        arot = mix("arot", [2, 8 * 2 * HALF_A])
        probsT = mix("probsT", [2, 4, P])
        kT_ret = at("kT_ret", sizes["probsT"], [2, P])
        kdec = at("kdec", sizes["probsT"] + KB, [256])
        score = at("score", sizes["probsT"] + 2 * KB, [RET_HEADS, P])
        qT_ret = mix("qT_ret", [2, 2, 2, P])
        stage = mix("stage", [2, W])
        assert MIX + 32 * KB <= sizes["stage"] <= MIX + 36 * KB
        state = mix("state", [2, 2, RET_V])
        qT_att = mix("qT_att", [2, 4, CHUNK])
        square = at("square", sizes["qT_att"], [512])
        aq = mix("aq", [2, 512])
        up_raw = at("up_raw", MIX, [2, NK * 256])
        up0_hi = at("up0_hi", MIX + 16 * KB, [NK, 256], f32r)
        up0_lo = at("up0_lo", MIX + 24 * KB, [NK, 256], f32r)
        down_raw = at("down_raw", MIX + 32 * KB, [2, MODEL])
        gains = at("gains", MIX + 40 * KB, [2, 2, W])
        gate_raw = at("gate_raw", MIX, [8, W])
        gw0_hi = at("gw0_hi", MIX + 16 * KB, [4, W], f32r)
        gw0_lo = at("gw0_lo", MIX + 24 * KB, [4, W], f32r)
        ple_raw = at("ple_raw", MIX + 32 * KB, [2, MODEL])

        decayT = cst[:, C_DECAY:C_IDENT].rearrange("p (h i) -> p h i", h=RET_HEADS)
        ident = cst[:, C_IDENT:C_QDEC]
        q_decay, k_decay = cst[:, C_QDEC:C_KDEC], cst[:, C_KDEC:C_SDEC]
        state_decay = cst[:, C_SDEC:C_FREQ]
        freq = cst[:, C_FREQ:C_MHALF]
        minus_half = cst[:, C_MHALF:C_END]
        cos_r, sin_r = trig[:, 0, :, 0:HALF_R], trig[:, 1, :, 0:HALF_R]
        cos_a, sin_a = trig[:, 0, :, HALF_R:NFREQ], trig[:, 1, :, HALF_R:NFREQ]

        posi = small[:, 0:8]
        posf = small[:, 8:16]
        sink = small[:, 16:20]
        rms = small[:, 32:40].rearrange("p (s h) -> p s h", s=2)
        smax = small[:, 40:48].rearrange("p (e b) -> p e b", e=2)
        sneg = small[:, 48:56].rearrange("p (e b) -> p e b", e=2)
        ssum = small[:, 56:64].rearrange("p (e b) -> p e b", e=2)
        sinkd = small[:, 64:72].rearrange("p (e b) -> p e b", e=2)
        sinke = small[:, 72:80].rearrange("p (e b) -> p e b", e=2)
        srec = small[:, 80:88].rearrange("p (e b) -> p e b", e=2)
        bnst = small[:, 96:120].rearrange("p (s n) -> p s n", s=2)
        mean = small[:, 128:144].rearrange("p (t n) -> p t n", t=NT)
        vare = small[:, 144:152]
        rstd = small[:, 152:160]
        nbias = small[:, 160:168]
        rsum = small[:, 168:176].rearrange("p (s h) -> p s h", s=2)

        psum = [ctx.enter_context(nc.psum_tensor(f"pair{j}", [P, 2 * W], fp32)) for j in range(4)]

        def bank(b):
            return psum[b // 2][:, (b % 2) * W:(b % 2 + 1) * W]

        def sem(name):
            return ctx.enter_context(nc.semaphore(name))

        cst_in_s, pos_in_s, conv_in_s = sem("cst_in"), sem("pos_in"), sem("conv_in")
        xT_in = [sem(f"xT_in{k}") for k in range(NK)] + [sem("xT_in0b")]
        w_in_s = [sem(f"w_in{j}") for j in range(RAWS)]
        xres_in = [sem(f"xres_in{j}") for j in range(2)]
        gains_in = sem("gains_in")
        up_in = [sem(f"up_in{f}") for f in range(2)]
        down_in = [sem(f"down_in{f}") for f in range(2)]
        gate_in = [sem(f"gate_in{j}") for j in range(8)]
        ple_in = sem("ple_in")
        out_s = [sem(f"out{j}") for j in range(2)]
        x_hi, x_lo = sem("x_hi"), sem("x_lo")
        w_hi, w_lo, w_used = sem("w_hi"), sem("w_lo"), sem("w_used")
        dense = sem("dense")
        taken = sem("taken")
        res_done = sem("res_done")
        dve_s = sem("dve")
        angle_s, sine_s, rot_s, arotk_s, arotq_s = (sem(n) for n in ("angle", "sine", "rot", "arotk", "arotq"))
        zero_s = sem("zero")
        rT, rT_out, kd_s, r_score, r_decayed, r_kv, r_state, r_y, r_yout, r_sq, r_gated = (
            sem(n) for n in ("rT", "rT_out", "kd", "r_score", "r_decayed", "r_kv", "r_state", "r_y",
                             "r_yout", "r_sq", "r_gated"))
        r_ms, r_rms = sem("r_ms"), sem("r_rms")
        akT, akT_out, veven_s = sem("akT"), sem("akT_out"), sem("veven")
        aqT, aqT_out, a_score, a_max, a_exp, a_prob, a_pT, a_pT_out, a_y = (
            sem(n) for n in ("aqT", "aqT_out", "a_score", "a_max", "a_exp", "a_prob", "a_pT", "a_pT_out", "a_y"))
        a_hi, a_lo, m_T, m_hi, m_lo = (sem(n) for n in ("a_hi", "a_lo", "m_T", "m_hi", "m_lo"))
        n_var, n_rstd, n_bias, n_z, n_gain, n_h, n_T, n_hi, n_lo, n_alpha = (
            sem(n) for n in ("n_var", "n_rstd", "n_bias", "n_z", "n_gain", "n_h", "n_T", "n_hi", "n_lo", "n_alpha"))
        up_hi_s, up_lo_s, dn_hi_s, dn_lo_s = (sem(n) for n in ("up_hi", "up_lo", "dn_hi", "dn_lo"))
        u_done, c_init, c_done, gelu_s, g_mul, g_hi, g_lo, d_done, d_added = (
            sem(n) for n in ("u_done", "c_init", "c_done", "gelu", "g_mul", "g_hi", "g_lo", "d_done", "d_added"))
        gw_hi, gw_lo, gw_lo_pool, gw_used = (sem(n) for n in ("gw_hi", "gw_lo", "gw_lo_pool", "gw_used"))
        pT_hi_s, pT_lo_s, pl_hi, pl_lo, pl_done = (sem(n) for n in ("pT_hi", "pT_lo", "pl_hi", "pl_lo", "pl_done"))
        gt_done, sig_s, gt_mul = sem("gt_done"), sem("sig"), sem("gt_mul")
        gt_add0, gt_add1 = sem("gt_add0"), sem("gt_add1")

        def f32(ap):
            return ap.bitcast(fp32)

        items = [(b, k) for b in BLOCKS for k in range(NK)]
        first_unit = {b: j * NT for j, b in enumerate(BLOCKS)}
        N_ACT_UNITS = 5 * NT
        OUT0, OUT1 = first_unit["out0"], first_unit["out1"]

        def tok(t, n=P):
            return slice(t * P, t * P + n)

        up_hi_t, up_lo_t = (up0_hi, up1_hi), (up0_lo, up1_lo)
        gw_hi_t, gw_lo_t = (gw0_hi, gw1_hi), (gw0_lo, gw1_lo)
        def gate_split(engine, n):
            if n in GATE_LO_POOL:
                engine.wait_ge(gw_lo_pool, GATE_LO_POOL.index(n) + 1)
            else:
                engine.wait_ge(gw_lo, n + 1 - (len(GATE_LO_POOL) if n >= NK else 0))

        block = ctx.enter_context(nc.Block())

        @block.sync
        def _(sp):
            def weight(n):
                b, k = items[n]
                c = COLS[b]
                if n >= RAWS:
                    sp.wait_ge(w_lo, n - RAWS + 1)
                if b.startswith("out"):
                    src = w_out[k * P:(k + 1) * P, int(b[3]) * W:(int(b[3]) + 1) * W]
                else:
                    c0 = sum(COLS[x] for x in BLOCKS[:BLOCKS.index(b)])
                    src = w_in[k * P:(k + 1) * P, c0:c0 + c]
                sp.dma_start(w_raw[:, n % RAWS, 0:c], src).then_inc(w_in_s[n % RAWS], 16)

            def residual(u):
                if u >= 2:
                    sp.wait_ge(res_done, u - 1)
                else:
                    sp.wait_ge(r_gated, NT)
                sp.dma_start(stage[:, u % 2, :], x[tok(u % NT), (u // NT) * W:(u // NT + 1) * W])\
                    .then_inc(xres_in[u % 2], 16)

            for k in range(NK):
                if k == 0:
                    weight(k)
                for j, toks in enumerate(HALVES if k == 0 else ALL):
                    sp.dma_start(xT_raw[:, k, toks], xT[k * P:(k + 1) * P, toks]).then_inc(xT_in[NK * j + k], 16)
                if k:
                    weight(k)
                if k == 2:
                    sp.dma_start(cst[:, :], cst_in).then_inc(cst_in_s, 16)
                    sp.dma_start(posi.bitcast(mybir.dt.int32), pos).then_inc(pos_in_s, 16)
                    sp.dma_start(sink, sinks).then_inc(pos_in_s, 16)
                    sp.dma_start(convp[:, :, :], conv).then_inc(conv_in_s, 16)
            for n in range(NK, OUT1):
                weight(n)
            residual(0)
            residual(1)
            for n in range(OUT1, OUT1 + 4):
                weight(n)
            for u in range(2, NT):
                residual(u)
            for n in range(OUT1 + 4, OUT1 + NK):
                weight(n)
            sp.wait_ge(a_lo, NT)
            for j in range(2):
                sp.dma_start(gains[:, j, :, :], ln[j].partition_broadcast(P)).then_inc(gains_in, 16)
            residual(NT)
            residual(NT + 1)
            for f in range(2):
                sp.dma_start(up_raw[:, f, :], ff_up[f]).then_inc(up_in[f], 16)
            for u in range(NT + 2, 2 * NT):
                residual(u)
            sp.wait_ge(res_done, 2 * NT)
            for f in range(2):
                sp.dma_start(down_raw[:, f, :], ff_down[f]).then_inc(down_in[f], 16)
            sp.wait_ge(n_h, NT)
            for j in range(2):
                sp.dma_start(gains[:, j, :, :], ln[2 + j].partition_broadcast(P)).then_inc(gains_in, 16)
            with sp.Fori(1, PAIRS) as i:
                for f in range(2):
                    sp.wait_ge(up_lo_s, i * 2 + (f - 1))
                    sp.dma_start(up_raw[:, f, :], ff_up[bass.ds(i * 2 + f, 1), :, :]
                                 .rearrange("o p n -> (o p) n")).then_inc(up_in[f], 16)
                for f in range(2):
                    sp.wait_ge(dn_lo_s, i * 2 + (f - 1))
                    sp.dma_start(down_raw[:, f, :], ff_down[bass.ds(i * 2 + f, 1), :, :]
                                 .rearrange("o p n -> (o p) n")).then_inc(down_in[f], 16)
            sp.wait_ge(up_lo_s, 2 * PAIRS)
            for k in range(NK):
                sp.dma_start(gate_raw[:, k, :], w_gate[k * P:(k + 1) * P, 0:W]).then_inc(gate_in[k], 16)
            sp.wait_ge(dn_lo_s, 2 * PAIRS)
            for k in range(2):
                sp.dma_start(ple_raw[:, k, :], w_ple[k * P:(k + 1) * P, :]).then_inc(ple_in, 16)
            sp.wait_ge(g_lo, 2 * PAIRS + 1)
            for k in range(2):
                sp.dma_start(pT_raw[:, k, :], pT[k * P:(k + 1) * P, :]).then_inc(ple_in, 16)
            for k in range(NK):
                gate_split(sp, k)
                sp.dma_start(gate_raw[:, k, :], w_gate[k * P:(k + 1) * P, W:2 * W]).then_inc(gate_in[k], 16)
            for u in range(2 * NT):
                h, t = divmod(u, NT)
                sp.wait_ge((gt_add0, gt_add1)[h], t + 1)
                sp.dma_start(out[tok(t), h * W:(h + 1) * W], outs[:, u % 2, :]).then_inc(out_s[u % 2], 16)
            for j in range(2):
                sp.wait_ge(out_s[j], 16 * NT)

        @block.tensor
        def _(pe):
            mm = nc.tensor.matmul

            def three(dst, a_h, a_l, b_h, b_l, first, last):
                mm(dst, a_h, b_h, start=first, stop=False)
                mm(dst, a_h, b_l, start=False, stop=False)
                return mm(dst, a_l, b_h, start=False, stop=last)

            def product(u, k, dst, n):
                t, c = u % NT, COLS[items[n][0]]
                return three(dst[:, 0:c], actT_hi[:, k, tok(t)], actT_lo[:, k, tok(t)],
                             ring_hi[:, n % RING, 0:c], ring_lo[:, n % RING, 0:c], k == 0, k == NK - 1)

            def unit(u, midway=None):
                b, t = u // NT, u % NT
                if u < NT + 2:
                    pe.wait_ge(taken, u - NT + 1)
                elif u - 2 < N_ACT_UNITS:
                    pe.wait_ge(taken, u - 1)
                else:
                    pe.wait_ge(res_done, u - 2 - OUT0 + 1)
                for k in range(NK):
                    n = b * NK + k
                    if t == 0:
                        pe.wait_ge(w_lo, n + 1)
                    if midway is not None and k == NK // 2:
                        midway()
                    last = product(u, k, bank(u % 2), n)
                    if t == NT - 1 and k < NK - 1:
                        last.then_inc(w_used, 1)
                last.then_inc(dense, 1)

            for k in range(NK):
                pe.wait_ge(w_lo, k + 1)
                pe.wait_ge(x_lo, k + 2 if k else 1)
                for t in range(NT):
                    if k == 0 and t == NT // 2:
                        pe.wait_ge(x_lo, 2)
                    last = product(t, k, bank(t), k)
                    if k == NK - 1:
                        last.then_inc(dense, 1)
                if k < NK - 1:
                    last.then_inc(w_used, 1)
            for b in ("v", "akv"):
                for t in range(NT):
                    unit(first_unit[b] + t)

            def transpose(dst, src):
                return nc.tensor.transpose(dst, src, ident)

            def ret_transpose(t):
                pe.wait_ge(rot_s, t + 1)
                if t:
                    pe.wait_ge(rT_out, t)
                for j in range(4):
                    last = transpose(bank(4)[:, tok(j)], rqk[:, t, tok(j)])
                last.then_inc(rT, 1)

            def ak_transpose(t):
                pe.wait_ge(arotk_s, t + 1)
                if t:
                    pe.wait_ge(akT_out, t)
                transpose(bank(3)[:, 0:P], akv[:, t, 0:P]).then_inc(akT, 1)

            def ret_scores(t):
                pe.wait_ge(rT_out, t + 1)
                if t:
                    pe.wait_ge(r_decayed, t)
                for p in range(2):
                    last = mm(bank(5)[:, p * 256:(p + 1) * 256], kT_ret[:, p, :],
                              qT_ret[:, t % 2, p, :, :], start=True, stop=True)
                last.then_inc(r_score, 1)
                if t < NT - 1:
                    pe.wait_ge(kd_s, t + 1)
                    if t:
                        pe.wait_ge(r_state, t)
                    for h in range(RET_HEADS):
                        p, s = divmod(h, 2)
                        last = mm(bank(6)[s * RET_QK:(s + 1) * RET_QK, tok(p)],
                                  kdec[:, h * RET_QK:(h + 1) * RET_QK], rvy[:, t, tok(h)],
                                  start=True, stop=True)
                    last.then_inc(r_kv, 1)

            def ret_output(t):
                pe.wait_ge(r_decayed, t + 1)
                if t:
                    pe.wait_ge(r_state, t)
                    pe.wait_ge(r_sq, t)
                for h in range(RET_HEADS):
                    p, s = divmod(h, 2)
                    last = mm(bank(7)[:, tok(h)], score[:, h, :], rvy[:, t, tok(h)], start=True, stop=t == 0)
                    if t:
                        last = mm(bank(7)[:, tok(h)], qT_ret[:, t % 2, p, s, :],
                                  state[:, t % 2, p, :], start=False, stop=True)
                last.then_inc(r_y, 1)

            def aq_transpose(t):
                pe.wait_ge(arotq_s, t + 1)
                if t:
                    pe.wait_ge(m_lo, t)
                for c in range(4):
                    last = transpose(bank(2)[:, tok(c)], aq[:, t % 2, tok(c)])
                last.then_inc(aqT, 1)

            def att_scores(t):
                pe.wait_ge(aqT_out, t + 1)
                if t:
                    pe.wait_ge(a_exp, 2 * t)
                else:
                    pe.wait_ge(akT_out, NT)
                    pe.wait_ge(r_decayed, NT)
                for e in range(2):
                    n = 2 * t + e
                    dst = bank(4 + e).rearrange("p (c g k) -> p c g k", c=2, g=KV_HEADS)
                    runs = [(0, n * CHUNK, CHUNK), (CHUNK, (n - 1) * CHUNK, CHUNK)] if e == 0 else \
                           [(0, (n - 1) * CHUNK, 2 * CHUNK)]
                    for cp in range(2):
                        for at_key, key, size in runs[:1] if n == 0 else runs:
                            last = mm(dst[:, cp, :, at_key:at_key + size],
                                      qT_att[:, e, 2 * cp:2 * cp + 2, :].rearrange("p c i -> p (c i)"),
                                      kT_att[:, :, key:key + size], start=True, stop=True)
                    last.then_inc(a_score, 1)

            def probs_transpose(t):
                for e in range(2):
                    pe.wait_ge(a_prob, 2 * t + e + 1)
                    if t:
                        pe.wait_ge(a_pT_out, 2 * t - 1 + e)
                    elif e:
                        pe.wait_ge(r_sq, NT)
                    else:
                        pe.wait_ge(r_state, NT - 1)
                    for b in range(4):
                        last = transpose(bank(6 + e)[:, tok(b)], probs[:, e, b, :])
                    last.then_inc(a_pT, 1)

            def att_output(t):
                pe.wait_ge(a_pT_out, 2 * t + 2)
                pe.wait_ge(veven_s, 2 * t + 1)
                if t:
                    pe.wait_ge(a_lo, t)
                for e in range(2):
                    pt = probsT[:, e, :, :].rearrange("p (c g) q -> p c g q", c=2)
                    for g in range(KV_HEADS):
                        v = akv[:, t, P + g * HEAD:P + (g + 1) * HEAD] if e else \
                            v_even[:, t, g * HEAD:(g + 1) * HEAD]
                        last = mm(bank(3)[g * HEAD:(g + 1) * HEAD, e * 256:(e + 1) * 256], v, pt[:, :, g, :],
                                  start=True, stop=True)
                last.then_inc(a_y, 1)

            def mix_transpose(t):
                pe.wait_ge(r_gated, t + 1)
                pe.wait_ge(aqT_out, t + 1)
                for h in range(RET_HEADS):
                    last = transpose(bank(2)[:, tok(h)], rvy[:, t, tok(h)])
                last.then_inc(m_T, 1)

            for t in range(NT):
                ret_transpose(t)
                ak_transpose(t)
                unit(first_unit["gate"] + t)
                ret_scores(t)
                if t:
                    ret_output(t - 1)
            for s in range(NT + 3):
                if s >= NT:
                    pe.wait_ge(m_lo, s - NT + 1)
                    pe.wait_ge(a_lo, s - NT + 1)
                unit(first_unit["aq"] + s, (lambda: aq_transpose(s - 1)) if 1 <= s <= NT else None)
                if s == 0:
                    ret_output(NT - 1)
                if s >= 3:
                    att_output(s - 3)
                if 1 <= s <= NT:
                    mix_transpose(s - 1)
                if 2 <= s <= NT + 1:
                    probs_transpose(s - 2)
                if 1 <= s <= NT:
                    att_scores(s - 1)
            for t in range(3, NT):
                pe.wait_ge(m_lo, t + 1)
                pe.wait_ge(a_lo, t + 1)
                unit(OUT0 + t)

            def norm_transpose(n):
                t, pair = n % NT, psum[2 + n % 2]
                pe.wait_ge(n_h, n + 1)
                if n >= 2:
                    pe.wait_ge(n_lo, n - 1)
                elif n == 0:
                    pe.wait_ge(a_exp, 2 * NT)
                else:
                    pe.wait_ge(a_pT_out, 2 * NT)
                for k in range(NK):
                    last = transpose(pair[:, tok(k)], res[:, k // 4, t, tok(k % 4)])
                last.then_inc(n_T, 1)

            for t in range(NT):
                unit(OUT1 + t)
                if 2 <= t < NT - 1:
                    norm_transpose(t - 2)

            def up_part(f, part, toks):
                w_h, w_l = up_hi_t[f], up_lo_t[f]
                cols = slice(part * P, (part + 1) * P)
                for k in range(NK):
                    last = three(psum[part][:, toks], w_h[:, k, cols], w_l[:, k, cols], actT_hi[:, k, toks],
                                 actT_lo[:, k, toks], k == 0, k == NK - 1)
                return last

            def up(f, i):
                pe.wait_ge(up_lo_s, i * 2 + (f + 1))
                for part in range(2):
                    pe.wait_ge(c_done, i * 4 + (2 * f + part - 1))
                    for toks in HALVES:
                        last = up_part(f, part, toks)
                    last.then_inc(u_done, 1)

            pe.wait_ge(up_lo_s, 1)
            pe.wait_ge(n_lo, 4)
            up_part(0, 1, HALVES[0])
            norm_transpose(NT - 3)
            pe.wait_ge(res_done, 2 * NT)
            up_part(0, 0, HALVES[0])
            norm_transpose(NT - 2)
            for ready in (NT - 2, NT):
                pe.wait_ge(n_lo, ready)
                for part in range(2):
                    last = up_part(0, part, slice((ready - 2) * P, ready * P))
                    if ready == NT:
                        last.then_inc(u_done, 1)
                    elif part == 0:
                        norm_transpose(NT - 1)
            pe.wait_ge(up_lo_s, 2)
            for part in range(2):
                pe.wait_ge(c_done, part + 1)
                for toks in HALVES:
                    last = up_part(1, part, toks)
                last.then_inc(u_done, 1)

            def down_unit(t, pair, tiles=(0, 1)):
                for half in range(2):
                    cols = slice(half * W, (half + 1) * W)
                    for f in tiles:
                        last = three(pair[:, cols], gT_hi[:, f, tok(t)], gT_lo[:, f, tok(t)],
                                     down_hi[:, f, cols], down_lo[:, f, cols], f == 0, f == 1)
                if f == 1:
                    last.then_inc(d_done, 1)

            def down_units(i, first):
                pe.wait_ge(g_lo, i * 2 + 2)
                pe.wait_ge(dn_lo_s, i * 2 + 2)
                for t in range(NT):
                    if t > 1 or not first:
                        pe.wait_ge(d_added, i * NT + (t - 1))
                    down_unit(t, psum[2 + t % 2])

            up(0, 1)
            down_units(0, True)
            up(1, 1)
            with pe.Fori(2, PAIRS) as i:
                up(0, i)
                down_units(i - 1, False)
                up(1, i)
            before = (PAIRS - 1) * NT
            pe.wait_ge(g_lo, 2 * PAIRS - 1)
            pe.wait_ge(dn_lo_s, 2 * PAIRS)
            pe.wait_ge(d_added, before)
            for t in range(4):
                if t >= 2:
                    pe.wait_ge(c_done, 4 * PAIRS - 3 + t)
                down_unit(t, psum[LAST_PAIRS[t]], (0,))
            for t in range(NT):
                if t % 4 == 0:
                    pe.wait_ge(g_lo, 2 * PAIRS + t // 4)
                if t < 4:
                    down_unit(t, psum[LAST_PAIRS[t]], (1,))
                else:
                    pe.wait_ge(d_added, before + 1 + max(j for j in range(t) if LAST_PAIRS[j] == LAST_PAIRS[t]))
                    down_unit(t, psum[LAST_PAIRS[t]])
                if t == NT - 2:
                    norm_transpose(NT)

            def gate_unit(u):
                h, t = divmod(u, NT)
                if u >= 2:
                    pe.wait_ge(sig_s, u - 1)
                else:
                    pe.wait_ge(d_added, PAIRS * NT - 2)
                if h == 0:
                    pe.wait_ge(n_lo, NT + t + 1)
                for k in range(NK):
                    if t == 0:
                        gate_split(pe, h * NK + k)
                    if k == NK // 2 and h == 0 and t + 1 < NT:
                        if t == 0:
                            pe.wait_ge(d_added, PAIRS * NT)
                        norm_transpose(NT + t + 1)
                    last = three(bank(u % 2), actT_hi[:, k, tok(t)], actT_lo[:, k, tok(t)],
                                 gw_hi_t[k // 4][:, k % 4, :], gw_lo_t[k // 4][:, k % 4, :],
                                 k == 0, k == NK - 1)
                    if t == NT - 1 and k < NK - 1:
                        last.then_inc(gw_used, 1)
                last.then_inc(gt_done, 1)

            def ple_unit(u):
                h, t = divmod(u, NT)
                if u >= 2:
                    pe.wait_ge(gt_mul, u - 1)
                elif u == 0:
                    pe.wait_ge(pT_lo_s, 2)
                    pe.wait_ge(pl_lo, 2)
                for k in range(2):
                    last = three(bank(2 + u % 2), pT_hi[:, k, tok(t)], pT_lo[:, k, tok(t)],
                                 ple_hi[:, k, h * W:(h + 1) * W], ple_lo[:, k, h * W:(h + 1) * W],
                                 k == 0, k == 1)
                last.then_inc(pl_done, 1)

            for u in range(2 * NT):
                gate_unit(u)
                if u:
                    ple_unit(u - 1)
            ple_unit(2 * NT - 1)

        @block.scalar
        def _(act):
            A = nc.scalar.activation

            def copy(dst, src):
                return A(dst, src, ACT.Copy)

            def used(n):
                b, k = divmod(n, NK)
                if k < NK - 1:
                    act.wait_ge(w_used, b * (NK - 1) + k + 1)
                else:
                    act.wait_ge(dense, (b + 1) * NT)

            def weight_hi(n):
                c = COLS[items[n][0]]
                act.wait_ge(w_in_s[n % RAWS], 16 * (n // RAWS + 1))
                if n >= RING:
                    used(n - RING)
                copy(ring_hi[:, n % RING, 0:c], w_raw[:, n % RAWS, 0:c]).then_inc(w_hi, 1)

            def next_weights(b, t):
                if b + 1 < len(BLOCKS):
                    for k in range(4, NK) if t == NT - 1 else [t - 1] if 1 <= t <= 4 else []:
                        weight_hi((b + 1) * NK + k)

            def take(u, dst, func=ACT.Copy):
                act.wait_ge(dense, u + 1)
                c = COLS[items[u][0]]
                A(dst, bank(u if u < NT else u % 2)[:, 0:c], func).then_inc(taken, 1)

            weight_hi(0)
            for k in range(NK):
                for j, toks in enumerate(HALVES if k == 0 else ALL):
                    act.wait_ge(xT_in[NK * j + k], 16)
                    copy(actT_hi[:, k, toks], xT_raw[:, k, toks]).then_inc(x_hi, 1)
                if k:
                    weight_hi(k)
            for n in range(NK, 2 * NK):
                weight_hi(n)
            for t in range(NT):
                take(t, rqk[:, t, :])
            act.wait_ge(angle_s, 1)
            A(trig[:, 1, :, :], trig[:, 1, :, :], ACT.Sin).then_inc(sine_s, 1)
            A(trig[:, 0, :, :], trig[:, 0, :, :], ACT.Sin, scale=0.5).then_inc(sine_s, 1)
            for t in range(NT):
                take(NT + t, rvy[:, t, :])
                next_weights(1, t)
            for t in range(NT):
                take(2 * NT + t, akv[:, t, :])
                next_weights(2, t)

            def ret_transposed(t):
                act.wait_ge(rT, t + 1)
                if t:
                    act.wait_ge(r_score, t)
                if t >= 2:
                    act.wait_ge(r_y, t - 1)
                if t == 0:
                    act.wait_ge(zero_s, 2)
                b4 = bank(4).rearrange("p (a j q) -> p a j q", a=2, j=2)
                copy(kT_ret[:, :, :], b4[:, 1, :, :])
                for s in range(2):
                    rows = slice(s * 64, (s + 1) * 64)
                    last = copy(qT_ret[rows, t % 2, :, s, :], b4[rows, 0, :, :])
                last.then_inc(rT_out, 1)

            def ret_out(t):
                act.wait_ge(r_y, t + 1)
                copy(rvy[:, t, :], bank(7)).then_inc(r_yout, 1)
                if t:
                    act.wait_ge(r_ms, t)
                A(square[:, :], bank(7), ACT.Square).then_inc(r_sq, 1)

            for t in range(NT):
                ret_transposed(t)
                if t >= 2:
                    act.wait_ge(r_gated, t - 1)
                take(3 * NT + t, stage[:, t % 2, :], ACT.Silu)
                next_weights(3, t)
                if t:
                    ret_out(t - 1)

            def aq_transposed(t):
                act.wait_ge(aqT, t + 1)
                act.wait_ge(a_score, 2 * t) if t else act.wait_ge(r_ms, NT)
                copy(qT_att[:, :, :, :].rearrange("p e c i -> p c e i"),
                     bank(2).rearrange("p (c e i) -> p c e i", c=4, e=2)).then_inc(aqT_out, 1)

            def att_hi(t):
                act.wait_ge(a_y, t + 1)
                for e in range(2):
                    last = copy(actT_hi[:, 4:8, t * P + e * CHUNK:t * P + (e + 1) * CHUNK],
                                bank(3)[:, e * 256:(e + 1) * 256].rearrange("p (c i) -> p c i", c=4))
                last.then_inc(a_hi, 1)

            def mix_hi(t):
                act.wait_ge(m_T, t + 1)
                copy(actT_hi[:, 0:4, tok(t)], bank(2).rearrange("p (h q) -> p h q", h=4)).then_inc(m_hi, 1)

            def probs_transposed(t):
                for e in range(2):
                    act.wait_ge(a_pT, 2 * t + e + 1)
                    if t:
                        act.wait_ge(a_y, t)
                    copy(probsT[:, e, :, :], bank(6 + e)).then_inc(a_pT_out, 1)

            def exps(t):
                for e in range(2):
                    n = 2 * t + e
                    keys = CHUNK if n == 0 else 2 * CHUNK
                    act.wait_ge(a_max, n + 1)
                    if n == 0:
                        act.wait_ge(zero_s, 4)
                    if t:
                        act.wait_ge(a_pT, 2 * (t - 1) + e + 1)
                    dst = bank(4 + e).rearrange("p (b k) -> p b k", b=4)
                    for b in range(4):
                        A(probs[:, e, b, 0:keys], dst[:, b, 0:keys], ACT.Exp, bias=sneg[:, e, b:b + 1],
                          scale=HEAD ** -0.5, accum_out=ssum[:, e, b:b + 1])
                    A(sinke[:, e, :], sinkd[:, e, :], ACT.Exp).then_inc(a_exp, 1)

            for s in range(NT + 3):
                if 1 <= s <= NT:
                    aq_transposed(s - 1)
                if s < NT:
                    take(4 * NT + s, aq[:, s % 2, :])
                    next_weights(4, s)
                else:
                    next_weights(5, s - NT)
                if s == 0:
                    ret_out(NT - 1)
                if s >= 3:
                    att_hi(s - 3)
                if 1 <= s <= NT:
                    mix_hi(s - 1)
                if 2 <= s <= NT + 1:
                    probs_transposed(s - 2)
                if 1 <= s <= NT:
                    exps(s - 1)
            for t in range(3, NT):
                next_weights(5, t)

            def norm_z(n):
                t = n % NT
                act.wait_ge(n_bias, n + 1)
                r = res[:, :, t, :]
                A(r, r, ACT.Identity, bias=nbias[:, t:t + 1], scale=rstd[:, t:t + 1]).then_inc(n_z, 1)

            def norm_hi(n):
                act.wait_ge(n_T, n + 1)
                copy(actT_hi[:, :, tok(n % NT)], psum[2 + n % 2][:, :].rearrange("p (k q) -> p k q", k=NK))\
                    .then_inc(n_hi, 1)

            def residual_scaled(n):
                r = res[:, :, n % NT, :]
                A(r, r, ACT.Copy, scale=ALPHA).then_inc(n_alpha, 1)

            def up_split_hi(f, i):
                act.wait_ge(up_in[f], i * 16 + 16)
                act.wait_ge(u_done, i * 4 + (2 * f - 2)) if not isinstance(i, int) or i else None
                copy(up_hi_t[f][:, :, :], up_raw[:, f, :].rearrange("p (k n) -> p k n", k=NK)).then_inc(up_hi_s, 1)

            for t in range(NT + 1):
                if t:
                    norm_z(t - 1)
                if t >= 2 and t < NT:
                    norm_hi(t - 2)
                    residual_scaled(t - 2)
                if t == 3:
                    act.wait_ge(dense, (len(BLOCKS) - 1) * NT)
                    up_split_hi(0, 0)
                if t == 5:
                    up_split_hi(1, 0)
            for n in (NT - 2, NT - 1):
                norm_hi(n)
                residual_scaled(n)

            def conv_first(f, i):
                for part in range(2):
                    act.wait_ge(u_done, i * 4 + (2 * f + part + 1))
                    if not (isinstance(i, int) and i == 0 and f == 0):
                        act.wait_ge(g_lo, i * 2 + f)
                    par = convp[:, bass.ds(i * 2 + f, 1), part * 4:part * 4 + 4].rearrange("p o n -> p (o n)")
                    A(conv_ab[:, part, :], psum[part][:, :], ACT.Identity, scale=par[:, 2:3], bias=par[:, 3:4])\
                        .then_inc(c_init, 1)

            def gelu(f, i, parts=ALL):
                act.wait_ge(c_done, i * 4 + (2 * f + 1))
                for toks in parts:
                    A(conv_ab[:, 0, toks], conv_ab[:, 0, toks], ACT.Gelu_apprx_tanh).then_inc(gelu_s, 1)

            def gated_hi(f, i, parts=ALL):
                if not (isinstance(i, int) and i == 0):
                    act.wait_ge(d_done, i * NT)
                for j, toks in enumerate(parts):
                    act.wait_ge(g_mul, i * 2 + (f + 1 + j))
                    copy(gT_hi[:, f, toks], conv_ab[:, 0, toks]).then_inc(g_hi, 1)

            def down_split_hi(f, i):
                act.wait_ge(down_in[f], i * 16 + 16)
                copy(down_hi[:, f, :], down_raw[:, f, :]).then_inc(dn_hi_s, 1)

            def gate_hi(n):
                k = n % NK
                act.wait_ge(gate_in[k], 16 * (n // NK + 1))
                if n >= NK:
                    act.wait_ge(gw_used, k + 1) if k < NK - 1 else act.wait_ge(gt_done, NT)
                elif k == 0:
                    act.wait_ge(u_done, 4 * PAIRS - 2)
                elif k == 4:
                    act.wait_ge(u_done, 4 * PAIRS)
                copy(gw_hi_t[k // 4][:, k % 4, :], gate_raw[:, k, :]).then_inc(gw_hi, 1)

            def turn(i, last):
                conv_first(0, i)
                gelu(0, i)
                if not last:
                    up_split_hi(0, i + 1)
                gated_hi(0, i)
                for f in range(2):
                    down_split_hi(f, i)
                if last:
                    for k in range(4):
                        gate_hi(k)
                conv_first(1, i)
                parts = HALVES if last else ALL
                gelu(1, i, parts)
                if not last:
                    up_split_hi(1, i + 1)
                gated_hi(1, i, parts)
                if last:
                    for k in range(4, NK):
                        gate_hi(k)

            act.wait_ge(conv_in_s, 16)
            act.wait_ge(dense, len(BLOCKS) * NT)
            turn(0, False)
            with act.Fori(1, PAIRS - 1) as i:
                turn(i, False)
            turn(PAIRS - 1, True)

            norm_z(NT)
            norm_z(NT + 1)
            norm_hi(NT)
            act.wait_ge(ple_in, 64)
            act.wait_ge(d_done, NT * PAIRS)
            for k in range(2):
                copy(pT_hi[:, k, :], pT_raw[:, k, :]).then_inc(pT_hi_s, 1)
            for u in range(2 * NT):
                h, t = divmod(u, NT)
                if h == 0:
                    if t + 2 < NT:
                        norm_z(NT + t + 2)
                    if t + 1 < NT:
                        norm_hi(NT + t + 1)
                    if t == 0:
                        for k in range(2):
                            copy(ple_hi[:, k, :], ple_raw[:, k, :]).then_inc(pl_hi, 1)
                    if t == NT - 1:
                        for k in range(NK):
                            gate_hi(NK + k)
                act.wait_ge(gt_done, u + 1)
                if u >= 2:
                    act.wait_ge(gt_mul, u - 1)
                else:
                    act.wait_ge(pT_lo_s, 2)
                A(sig[:, u % 2, :], bank(u % 2), ACT.Sigmoid).then_inc(sig_s, 1)

        @block.vector
        def _(dve):
            V = nc.vector
            steps = {"n": 0, "loop": None}

            def own(ins):
                ins.then_inc(dve_s, 1)
                steps["n"] += 1

            def settle():
                n = steps["n"]
                dve.wait_ge(dve_s, n if steps["loop"] is None else steps["loop"] + n)

            def subtract_lo(dst, src, hi):
                return V.tensor_tensor(dst, src, f32(hi), ALU.subtract)

            def weight_lo(n):
                c = COLS[items[n][0]]
                dve.wait_ge(w_hi, n + 1)
                subtract_lo(ring_lo[:, n % RING, 0:c], w_raw[:, n % RAWS, 0:c], ring_hi[:, n % RING, 0:c])\
                    .then_inc(w_lo, 1)

            def next_weights(b, t):
                if b + 1 < len(BLOCKS):
                    for k in range(4, NK) if t == NT - 1 else [t - 1] if 1 <= t <= 4 else []:
                        weight_lo((b + 1) * NK + k)

            weight_lo(0)
            for k in range(NK):
                for j, toks in enumerate(HALVES if k == 0 else ALL):
                    dve.wait_ge(x_hi, k + 2 if k else j + 1)
                    subtract_lo(actT_lo[:, k, toks], xT_raw[:, k, toks], actT_hi[:, k, toks]).then_inc(x_lo, 1)
                if k:
                    weight_lo(k)
            for n in range(NK, 2 * NK):
                weight_lo(n)

            dve.wait_ge(cst_in_s, 16)
            dve.wait_ge(pos_in_s, 32)
            n_all = NT * NFREQ
            tmp = rot[:, :, 0:n_all].rearrange("p a (t f) -> p a t f", t=NT)
            ang, n_lo_t, n_hi_t = trig[:, 1, :, :], tmp[:, 0], tmp[:, 1]
            own(V.tensor_copy(posf, posi.bitcast(mybir.dt.int32)))
            settle()
            own(V.tensor_tensor(ang, posf.unsqueeze(2).to_broadcast([P, NT, NFREQ]),
                                freq.unsqueeze(1).to_broadcast([P, NT, NFREQ]), ALU.mult))
            settle()
            own(V.tensor_scalar(n_lo_t, ang, 1.0 / (2 * np.pi), ANGLE_MAGIC, ALU.mult, ALU.add))
            settle()
            own(V.tensor_scalar(n_lo_t, n_lo_t, ANGLE_MAGIC, None, ALU.subtract))
            settle()
            own(V.tensor_scalar(n_hi_t, n_lo_t, 2.0 ** -11, ANGLE_MAGIC, ALU.mult, ALU.add))
            settle()
            own(V.tensor_scalar(n_hi_t, n_hi_t, ANGLE_MAGIC, 2.0 ** 11, ALU.subtract, ALU.mult))
            settle()
            own(V.tensor_tensor(n_lo_t, n_lo_t, n_hi_t, ALU.subtract))
            settle()
            for part in TWO_PI:
                for n_part in (n_hi_t, n_lo_t):
                    own(V.scalar_tensor_tensor(out=ang, in0=n_part, scalar=-part, in1=ang, op0=ALU.mult, op1=ALU.add))
                    settle()
            own(V.tensor_scalar(ang, ang, PI_BELOW, -PI_BELOW, ALU.min, ALU.max))
            settle()
            V.tensor_copy(trig[:, 0, :, :], ang).then_inc(angle_s, 1)
            dve.wait_ge(sine_s, 2)
            cosines = trig[:, 0, :, :]
            own(V.tensor_tensor(cosines, cosines, cosines, ALU.mult))
            settle()
            own(V.tensor_scalar(cosines, cosines, -2.0, 1.0, ALU.mult, ALU.add))
            settle()

            def rotary(view, cos, sin, buf, heads, half):
                shape = [P, heads, 2, half]
                c = cos.unsqueeze(1).unsqueeze(1).to_broadcast(shape)
                s = sin.unsqueeze(1).unsqueeze(1).to_broadcast(shape)
                by_cos = buf[:, 0, 0:heads * 2 * half].rearrange("p (n a h) -> p n a h", n=heads, a=2)
                by_sin = buf[:, 1, 0:heads * 2 * half].rearrange("p (n a h) -> p n a h", n=heads, a=2)
                own(V.tensor_tensor(by_cos, view, c, ALU.mult))
                own(V.tensor_tensor(by_sin, view, s, ALU.mult))
                settle()
                own(V.tensor_tensor(view[:, :, 0, :], by_cos[:, :, 0, :], by_sin[:, :, 1, :], ALU.subtract))
                last = V.tensor_tensor(view[:, :, 1, :], by_cos[:, :, 1, :], by_sin[:, :, 0, :], ALU.add)
                return last

            def ret_rotary(t):
                dve.wait_ge(taken, t + 1)
                if t:
                    dve.wait_ge(rot_s, t)
                view = rqk[:, t, :].rearrange("p (n a h) -> p n a h", n=2 * RET_HEADS, a=2)
                own(rotary(view, cos_r[:, t, :], sin_r[:, t, :], rot, 2 * RET_HEADS, HALF_R))
                settle()
                q = rqk[:, t, 0:256].rearrange("p (h d) -> p h d", h=RET_HEADS)
                V.tensor_tensor(q, q, q_decay.unsqueeze(2).to_broadcast([P, RET_HEADS, RET_QK]), ALU.mult)\
                    .then_inc(rot_s, 1)

            for t in range(NT):
                ret_rotary(t)
                next_weights(1, t)
            for t in range(NT):
                dve.wait_ge(taken, 2 * NT + t + 1)
                if t:
                    dve.wait_ge(arotk_s, t)
                view = akv[:, t, 0:P].rearrange("p (n d) -> p n d", n=KV_HEADS)[:, :, 0:ROPE_DIM]\
                    .rearrange("p n (a h) -> p n a h", a=2)
                rotary(view, cos_a[:, t, :], sin_a[:, t, :], arot, KV_HEADS, HALF_A).then_inc(arotk_s, 1)
                next_weights(2, t)

            def ret_gate(t):
                dve.wait_ge(r_rms, t + 1)
                dve.wait_ge(taken, 3 * NT + t + 1)
                for h in range(RET_HEADS):
                    y = rvy[:, t, tok(h)]
                    last = V.scalar_tensor_tensor(out=y, in0=y, scalar=rms[:, t % 2, h:h + 1],
                                                  in1=stage[:, t % 2, tok(h)], op0=ALU.mult, op1=ALU.mult)
                last.then_inc(r_gated, 1)

            def ret_square_sum(t):
                dve.wait_ge(r_sq, t + 1)
                if t >= 2:
                    dve.wait_ge(r_rms, t - 1)
                own(V.reduce_sum(rsum[:, t % 2, :], square[:, :].rearrange("p (h e) -> p h e", h=RET_HEADS), AX.X))
                settle()
                V.tensor_scalar(rsum[:, t % 2, :], rsum[:, t % 2, :], 1.0 / RET_V, RMS_EPS, ALU.mult, ALU.add)\
                    .then_inc(r_ms, 1)

            for t in range(NT):
                if t >= 2:
                    ret_gate(t - 2)
                if t < NT - 1:
                    if t:
                        dve.wait_ge(r_kv, t)
                    dve.wait_ge(rot_s, t + 1)
                    k = rqk[:, t, 256:512].rearrange("p (h d) -> p h d", h=RET_HEADS)
                    V.tensor_tensor(kdec[:, :].rearrange("p (h d) -> p h d", h=RET_HEADS), k,
                                    k_decay.unsqueeze(2).to_broadcast([P, RET_HEADS, RET_QK]), ALU.mult)\
                        .then_inc(kd_s, 1)
                dve.wait_ge(akT, t + 1)
                if t == 0:
                    dve.wait_ge(zero_s, 2)
                for g in range(KV_HEADS):
                    rows = slice(g * HEAD, (g + 1) * HEAD)
                    last = V.tensor_copy(kT_att[rows, g, tok(t)], bank(3)[rows, 0:P])
                last.then_inc(akT_out, 1)
                next_weights(3, t)
                dve.wait_ge(r_score, t + 1)
                if t:
                    dve.wait_ge(r_y, t)
                V.tensor_tensor(score[:, :, :], bank(5).rearrange("p (h q) -> p h q", h=RET_HEADS), decayT, ALU.mult)\
                    .then_inc(r_decayed, 1)
                if t < NT - 1:
                    dve.wait_ge(r_kv, t + 1)
                    for p in range(2):
                        dst, kv = state[:, (t + 1) % 2, p, :], bank(6)[:, tok(p)]
                        if t == 0:
                            last = V.tensor_copy(dst, kv)
                        else:
                            if p == 0:
                                dve.wait_ge(r_state, t)
                            last = V.scalar_tensor_tensor(out=dst, in0=state[:, t % 2, p, :],
                                                          scalar=state_decay[:, p:p + 1], in1=kv,
                                                          op0=ALU.mult, op1=ALU.add)
                    last.then_inc(r_state, 1)
                if t:
                    ret_square_sum(t - 1)

            def att_max(t):
                for e in range(2):
                    n = 2 * t + e
                    keys = CHUNK if n == 0 else 2 * CHUNK
                    dve.wait_ge(a_score, n + 1)
                    s = bank(4 + e).rearrange("p (b k) -> p b k", b=4)[:, :, 0:keys]
                    own(V.reduce_max(smax[:, e, :], s, AX.X))
                    settle()
                    own(V.scalar_tensor_tensor(out=smax[:, e, :], in0=smax[:, e, :], scalar=HEAD ** -0.5,
                                               in1=sink, op0=ALU.mult, op1=ALU.max))
                    settle()
                    own(V.tensor_tensor(sinkd[:, e, :], sink, smax[:, e, :], ALU.subtract))
                    V.tensor_scalar(sneg[:, e, :], smax[:, e, :], -1.0, None, ALU.mult).then_inc(a_max, 1)

            def att_normalise(t):
                for e in range(2):
                    dve.wait_ge(a_exp, 2 * t + e + 1)
                    own(V.tensor_tensor(srec[:, e, :], ssum[:, e, :], sinke[:, e, :], ALU.add))
                    settle()
                    own(V.reciprocal(srec[:, e, :], srec[:, e, :]))
                    settle()
                    V.tensor_tensor(probs[:, e, :, :], probs[:, e, :, :],
                                    srec[:, e, :].unsqueeze(2).to_broadcast([P, 4, P]), ALU.mult).then_inc(a_prob, 1)

            def residual_add(u):
                h, t = divmod(u, NT)
                dve.wait_ge(dense, OUT0 + u + 1)
                dve.wait_ge(xres_in[u % 2], 16 * (u // 2 + 1))
                V.scalar_tensor_tensor(out=res[:, h, t, :], in0=stage[:, u % 2, :], scalar=ALPHA,
                                       in1=bank(u % 2), op0=ALU.mult, op1=ALU.add).then_inc(res_done, 1)

            for s in range(NT + 3):
                if s == 0:
                    ret_gate(NT - 2)
                    ret_square_sum(NT - 1)
                if s == 1:
                    ret_gate(NT - 1)
                if s < NT:
                    dve.wait_ge(taken, 4 * NT + s + 1)
                    dve.wait_ge(arotq_s, s) if s else dve.wait_ge(arotk_s, NT)
                    view = aq[:, s % 2, :].rearrange("p (n d) -> p n d", n=Q_HEADS)[:, :, 0:ROPE_DIM]\
                        .rearrange("p n (a h) -> p n a h", a=2)
                    rotary(view, cos_a[:, s, :], sin_a[:, s, :], arot, Q_HEADS, HALF_A).then_inc(arotq_s, 1)
                    next_weights(4, s)
                else:
                    residual_add(s - NT)
                    next_weights(5, s - NT)
                if s >= 3:
                    t = s - 3
                    dve.wait_ge(a_hi, t + 1)
                    for e in range(2):
                        cols = slice(t * P + e * CHUNK, t * P + (e + 1) * CHUNK)
                        last = subtract_lo(actT_lo[:, 4:8, cols],
                                           bank(3)[:, e * 256:(e + 1) * 256].rearrange("p (c i) -> p c i", c=4),
                                           actT_hi[:, 4:8, cols])
                    last.then_inc(a_lo, 1)
                if 1 <= s <= NT:
                    t = s - 1
                    dve.wait_ge(m_hi, t + 1)
                    subtract_lo(actT_lo[:, 0:4, tok(t)], bank(2).rearrange("p (h q) -> p h q", h=4),
                                actT_hi[:, 0:4, tok(t)]).then_inc(m_lo, 1)
                    att_max(t)
                    att_normalise(t)
            for t in range(3, NT):
                residual_add(t)
                next_weights(5, t)

            def norm_stats(n):
                t, s = n % NT, n % 2
                for h in range(2):
                    own(V.bn_stats(bnst[:, s, 6 * h:6 * h + 6], res[:, h, t, :]))
                settle()
                own(V.bn_aggr(mean[:, t, :], bnst[:, s, :]))
                settle()
                V.tensor_scalar(vare[:, t:t + 1], mean[:, t, 1:2], LN_EPS, None, ALU.add).then_inc(n_var, 1)

            def norm_bias(n):
                t = n % NT
                dve.wait_ge(n_rstd, n + 1)
                V.tensor_scalar(nbias[:, t:t + 1], mean[:, t, 0:1], rstd[:, t:t + 1], -1.0, ALU.mult, ALU.mult)\
                    .then_inc(n_bias, 1)

            def norm_gain(n):
                dve.wait_ge(n_z, n + 1)
                dve.wait_ge(gains_in, 32 if n < NT else 64)
                r = res[:, :, n % NT, :]
                V.tensor_tensor(r, r, gains[:, 0, :, :], ALU.mult).then_inc(n_gain, 1)

            def norm_lo(n):
                dve.wait_ge(n_hi, n + 1)
                subtract_lo(actT_lo[:, :, tok(n % NT)], psum[2 + n % 2][:, :].rearrange("p (k q) -> p k q", k=NK),
                            actT_hi[:, :, tok(n % NT)]).then_inc(n_lo, 1)

            def up_split_lo(f, i):
                dve.wait_ge(up_hi_s, i * 2 + (f + 1))
                subtract_lo(up_lo_t[f][:, :, :], up_raw[:, f, :].rearrange("p (k n) -> p k n", k=NK),
                            up_hi_t[f][:, :, :]).then_inc(up_lo_s, 1)

            for t in range(NT + 1):
                if t:
                    norm_bias(t - 1)
                if t == NT:
                    norm_lo(NT - 3)
                if t < NT:
                    residual_add(NT + t)
                if t:
                    norm_gain(t - 1)
                if t < NT:
                    dve.wait_ge(res_done, NT + t + 1)
                    norm_stats(t)
                if 2 <= t < NT - 1:
                    norm_lo(t - 2)
                if t == 3:
                    up_split_lo(0, 0)
                if t == 5:
                    up_split_lo(1, 0)
            for n in (NT - 2, NT - 1):
                norm_lo(n)

            def conv_taps(f, i, midway=None):
                for part in range(2):
                    dve.wait_ge(c_init, i * 4 + (2 * f + part + 1))
                    par = convp[:, bass.ds(i * 2 + f, 1), part * 4:part * 4 + 4].rearrange("p o n -> p (o n)")
                    for back in (1, 2):
                        c, u = conv_ab[:, part, back:TOKENS], psum[part][:, 0:TOKENS - back]
                        ins = V.scalar_tensor_tensor(out=c, in0=u, scalar=par[:, 2 - back:3 - back], in1=c,
                                                     op0=ALU.mult, op1=ALU.add)
                        if back == 1:
                            own(ins)
                            if part and midway is not None:
                                midway()
                            settle()
                    ins.then_inc(c_done, 1)

            def gated(f, i, parts=ALL):
                dve.wait_ge(c_done, i * 4 + (2 * f + 2))
                for j, toks in enumerate(parts):
                    dve.wait_ge(gelu_s, i * 2 + (f + 1 + j))
                    a, b = conv_ab[:, 0, toks], conv_ab[:, 1, toks]
                    V.tensor_tensor(a, a, b, ALU.mult).then_inc(g_mul, 1)
                for j, toks in enumerate(parts):
                    dve.wait_ge(g_hi, i * 2 + (f + 1 + j))
                    subtract_lo(gT_lo[:, f, toks], conv_ab[:, 0, toks], gT_hi[:, f, toks]).then_inc(g_lo, 1)

            def down_split_lo(f, i):
                dve.wait_ge(dn_hi_s, i * 2 + (f + 1))
                subtract_lo(down_lo[:, f, :], down_raw[:, f, :], down_hi[:, f, :]).then_inc(dn_lo_s, 1)

            def down_add(i, t, pair):
                dve.wait_ge(d_done, i * NT + (t + 1))
                r = res[:, :, t, :]
                V.tensor_tensor(r, r, psum[pair][:, :].rearrange("p (h n) -> p h n", h=2), ALU.add)\
                    .then_inc(d_added, 1)

            def gate_lo(n):
                k = n % NK
                dve.wait_ge(gw_hi, n + 1)
                subtract_lo(gw_lo_t[k // 4][:, k % 4, :], gate_raw[:, k, :], gw_hi_t[k // 4][:, k % 4, :])\
                    .then_inc(gw_lo, 1)

            def turn(i, first, last):
                conv_taps(0, i, None if first else lambda: down_add(i - 1, 0, 2))
                if not first:
                    for t in range(1, NT):
                        down_add(i - 1, t, 2 + t % 2)
                if not last:
                    up_split_lo(0, i + 1)
                gated(0, i)
                for f in range(2):
                    down_split_lo(f, i)
                if last:
                    for k in range(4):
                        gate_lo(k)
                conv_taps(1, i)
                if not last:
                    up_split_lo(1, i + 1)
                gated(1, i, HALVES if last else ALL)
                if last:
                    for k in range(4, GATE_LO_POOL[0]):
                        gate_lo(k)

            dve.wait_ge(n_alpha, NT)
            turn(0, True, False)
            own_per_turn, before = 4, steps["n"]
            with dve.Fori(1, PAIRS - 1) as i:
                steps["loop"], steps["n"] = i * own_per_turn, before - own_per_turn
                turn(i, False, False)
            assert steps["n"] == before
            steps["loop"], steps["n"] = None, before + own_per_turn * (PAIRS - 2)
            turn(PAIRS - 1, False, True)

            def stats(t):
                dve.wait_ge(d_added, (PAIRS - 1) * NT + t + 1)
                norm_stats(NT + t)

            def add(*tiles):
                for t in tiles:
                    down_add(PAIRS - 1, t, LAST_PAIRS[t])

            add(0)
            stats(0)
            add(1)
            norm_bias(NT)
            add(2)
            norm_gain(NT)
            stats(1)
            add(3, 4)
            norm_bias(NT + 1)
            add(5)
            norm_gain(NT + 1)
            add(6)
            norm_lo(NT)
            stats(2)
            add(7)

            def gate_mul(u):
                h, t = divmod(u, NT)
                dve.wait_ge(pl_done, u + 1)
                dve.wait_ge(sig_s, u + 1)
                if u >= 2:
                    dve.wait_ge(out_s[u % 2], 16 * (u // 2))
                o = outs[:, u % 2, :]
                V.tensor_tensor(o, bank(2 + u % 2), sig[:, u % 2, :], ALU.mult).then_inc(gt_mul, 1)
                if h:
                    dve.wait_ge(gt_mul, u + 1)
                    V.tensor_tensor(o, o, res[:, h, t, :], ALU.add).then_inc(gt_add1, 1)

            for t in range(NT):
                if t + 2 < NT:
                    norm_bias(NT + t + 2)
                if t + 3 < NT:
                    stats(t + 3)
                if t + 2 < NT:
                    norm_gain(NT + t + 2)
                if t + 1 < NT:
                    norm_lo(NT + t + 1)
                if t == 0:
                    for k in range(2):
                        dve.wait_ge(pl_hi, k + 1)
                        subtract_lo(ple_lo[:, k, :], ple_raw[:, k, :], ple_hi[:, k, :]).then_inc(pl_lo, 1)
                if t == NT - 1:
                    for k in range(NK):
                        gate_lo(NK + k)
                if t:
                    gate_mul(t - 1)
            for u in range(NT - 1, 2 * NT):
                gate_mul(u)

        @block.gpsimd
        def _(pool):
            G = nc.gpsimd
            G.memset(qT_ret[:, :, :, :, :], 0.0).then_inc(zero_s, 1)
            G.memset(kT_att[:, :, :], 0.0).then_inc(zero_s, 1)
            G.memset(v_even[:, 0, :], 0.0).then_inc(zero_s, 1)
            pool.wait_ge(zero_s, 3)
            for t in range(NT):
                pool.wait_ge(taken, 2 * NT + t + 1)
                own_rows, next_rows = slice(0, CHUNK), slice(CHUNK, P)
                G.tensor_copy(v_even[own_rows, t, :], akv[own_rows, t, P:2 * P]).then_inc(veven_s, 1)
                pool.wait_ge(veven_s, 2 * t + 1)
                if t < NT - 1:
                    G.tensor_copy(v_even[next_rows, t + 1, :], akv[next_rows, t, P:2 * P]).then_inc(veven_s, 1)
                    pool.wait_ge(veven_s, 2 * t + 2)
            for t in range(NT):
                pool.wait_ge(r_ms, t + 1)
                if t >= 2:
                    pool.wait_ge(r_gated, t - 1)
                G.tensor_tensor(rms[:, t % 2, :], rsum[:, t % 2, :], minus_half, ALU.pow).then_inc(r_rms, 1)
                if t == 1:
                    pool.wait_ge(rot_s, NT)
                    G.memset(probs[:, 0, :, CHUNK:P], 0.0).then_inc(zero_s, 1)

            def norm_add(n):
                pool.wait_ge(n_gain, n + 1)
                r = res[:, :, n % NT, :]
                G.tensor_tensor(r, r, gains[:, 1, :, :], ALU.add).then_inc(n_h, 1)

            def gate_add(u):
                pool.wait_ge(gt_mul, u + 1)
                o = outs[:, u % 2, :]
                G.tensor_tensor(o, o, res[:, 0, u, :], ALU.add).then_inc(gt_add0, 1)

            def norm_rstd(n):
                t = n % NT
                pool.wait_ge(n_var, n + 1)
                G.tensor_tensor(rstd[:, t:t + 1], vare[:, t:t + 1], minus_half[:, 0:1], ALU.pow)\
                    .then_inc(n_rstd, 1)

            norm_rstd(0)
            for n in range(1, NT - 1):
                norm_add(n - 1)
                norm_rstd(n)
            norm_rstd(NT - 1)
            norm_add(NT - 2)
            norm_add(NT - 1)
            for k in GATE_LO_POOL:
                pool.wait_ge(gw_hi, k + 1)
                G.tensor_tensor(gw_lo_t[k // 4][:, k % 4, :], gate_raw[:, k, :],
                                f32(gw_hi_t[k // 4][:, k % 4, :]), ALU.subtract).then_inc(gw_lo_pool, 1)
            norm_rstd(NT)
            for t in range(NT):
                norm_add(NT + t)
                if t + 1 < NT:
                    norm_rstd(NT + t + 1)
                if t == 1:
                    for k in range(2):
                        pool.wait_ge(pT_hi_s, k + 1)
                        G.tensor_tensor(pT_lo[:, k, :], pT_raw[:, k, :], f32(pT_hi[:, k, :]), ALU.subtract)\
                            .then_inc(pT_lo_s, 1)
                if t >= NT // 2:
                    gate_add(t - NT // 2)
            for u in range(NT // 2, NT):
                gate_add(u)


def retention_constants():
    gamma = 1.0 - 2.0 ** (-5.0 - np.arange(RET_HEADS))
    i, j = np.arange(P)[None, :], np.arange(P)[:, None]
    same, later = i // CHUNK == j // CHUNK, i // CHUNK > j // CHUNK
    c = np.zeros((P, C_END), np.float64)
    scale = RET_QK ** -0.5
    for h, g in enumerate(gamma):
        d = np.where(same, g ** np.abs(i - j), np.where(later, g ** np.maximum(i - j, 0), 0.0))
        c[:, C_DECAY + h * P:C_DECAY + (h + 1) * P] = d * g ** -(i + 1.0) * scale
        c[:, C_QDEC + h] = g ** (np.arange(P) + 1.0)
        c[:, C_KDEC + h] = g ** (P - 1.0 - np.arange(P)) * scale
    for p in range(2):
        c[:64, C_SDEC + p], c[64:, C_SDEC + p] = gamma[2 * p] ** P, gamma[2 * p + 1] ** P
    c[:, C_IDENT:C_QDEC] = np.eye(P)
    c = c.astype(np.float32)
    ret = 10000.0 ** -(np.arange(HALF_R, dtype=np.float32) * np.float32(1 / (HALF_R - 1))).astype(np.float64)
    att = 500000.0 ** -(np.arange(HALF_A, dtype=np.float32) / HALF_A).astype(np.float64)
    c[:, C_FREQ:C_FREQ + HALF_R], c[:, C_FREQ + HALF_R:C_MHALF] = ret, att
    c[:, C_MHALF:C_END] = -0.5
    return c


def kernel(x, p, positions, w_in, w_out, attn_sinks, ln1_g, ln1_b, w_up, conv_w, conv_b,
           w_down, ln2_g, ln2_b, w_ple_gate, w_ple_proj):
    import concourse.bacc as bacc
    from concourse.bass_utils import run_bass_kernel_spmd

    a = np.ascontiguousarray
    x, p, w_in, w_out = np.asarray(x)[0], np.asarray(p)[0, 0], np.asarray(w_in)[0], np.asarray(w_out)[0]
    w_up, w_down = np.asarray(w_up)[0], np.asarray(w_down)[0]
    conv_w, conv_b = np.asarray(conv_w)[0], np.asarray(conv_b)[0]
    heads = np.arange(Q_HEADS * HEAD).reshape(KV_HEADS, 4, HEAD).transpose(1, 0, 2).reshape(-1)
    qk, v, g = np.arange(512), np.arange(512, 1024), np.arange(1024, 1536)
    aq, akv = 1536 + heads, np.arange(2048, 2304)
    w_in = w_in[:, np.concatenate([qk, v, akv, g, aq])]
    w_out = w_out[np.concatenate([np.arange(512), 512 + heads]), :]
    sinks = np.asarray(attn_sinks)[0].reshape(KV_HEADS, 2, 2)
    sinks = np.repeat(sinks.transpose(2, 1, 0).reshape(2, 4), CHUNK, axis=0)
    up = w_up.reshape(NK, P, 2, NF, P).transpose(3, 1, 0, 2, 4).reshape(NF, P, NK * 256)
    down = w_down.reshape(NF, P, MODEL)
    conv = np.concatenate([conv_w, conv_b[None]], 0).reshape(4, 2, NF, P).transpose(3, 2, 1, 0).reshape(P, NF, 8)
    ln = np.stack([np.asarray(t)[0] for t in (ln1_g, ln1_b, ln2_g, ln2_b)]).reshape(4, 2, W)
    ins = {
        "xT": x.T, "x": x, "pT": p.T, "pos": np.asarray(positions)[0].reshape(NT, P).T,
        "w_in": w_in, "w_out": w_out, "sinks": sinks, "ln": ln, "ff_up": up, "ff_down": down,
        "conv": conv, "w_gate": np.asarray(w_ple_gate)[0], "w_ple": np.asarray(w_ple_proj)[0],
        "cst_in": retention_constants(),
    }
    nc = bacc.Bacc("TRN2", target_bir_lowering=False, num_devices=1)
    arrays, args = {}, {}
    for name, t in ins.items():
        t = a(t)
        arrays[f"{name}_dram"] = t
        args[name] = nc.dram_tensor(f"{name}_dram", t.shape, mybir.dt.from_np(t.dtype), kind="ExternalInput").ap()
    args["out"] = nc.dram_tensor("out_dram", (TOKENS, MODEL), mybir.dt.float32, kind="ExternalOutput").ap()
    build(nc, **args)
    r = run_bass_kernel_spmd(nc, [arrays], core_ids=[0])
    return r.results[0]["out_dram"].reshape(1, TOKENS, MODEL)
```
